# Optimizing a Trainium2 kernel written in Bass

```python
import math
import jax
import jax.numpy as jnp
from jax import lax
import numpy as np
import jax, jax.numpy as jnp

D_MODEL = 1024
BATCH = 1
SEQ = 512
DEPTH = 1

HEAD_DIM = 64
Q_BLOCK = 128

A_HEADS = 4
A_PATTERNS = ((128, 1), (512, 4), (2048, 16))
A_GROUPS = 3
A_WIDTH = A_HEADS * HEAD_DIM

B_HEADS = 4
B_WIDTH = B_HEADS * HEAD_DIM
IDX_HEADS = 4
IDX_DIM = 64
TOPK_MAX = 256

C_HEADS = 4
C_WIDTH = C_HEADS * HEAD_DIM
C_LORA_W = 32
C_LORA_A = 32
C_LORA_G = 64
C_LORA_V = 16
C_IN = 3 * C_WIDTH + C_LORA_W + C_LORA_A + C_LORA_G
C_GN_EPS = 64e-5

D_HEADS = 4
D_INNER = D_HEADS * HEAD_DIM
D_GROUPS = 2
D_STATE = 64
D_CONV = 4
D_CHUNK = 128
D_XBC = D_INNER + 2 * D_GROUPS * D_STATE
D_NORM_EPS = 1e-5

N_BRANCH = 4
BRANCH_WIDTH = 256

N_EXPERT_GROUPS = 4
EXPERTS_PER_GROUP = 8
N_EXPERTS = N_EXPERT_GROUPS * EXPERTS_PER_GROUP
TOP_K_EXPERTS = 2
D_EXPERT = 512
MOE_BLOCK = 128

LN_EPS = 1e-5
DEEPNORM_ALPHA = (2 * DEPTH) ** 0.25
DEEPNORM_BETA = (8 * DEPTH) ** -0.25

IN_SEGMENTS = (
    ('a_qkv', 3 * A_GROUPS * A_WIDTH),
    ('b_qkv', 3 * B_WIDTH),
    ('b_idx_q', IDX_HEADS * IDX_DIM),
    ('b_idx_k', IDX_DIM),
    ('b_idx_w', IDX_HEADS),
    ('c_in', C_IN),
    ('d_z', D_INNER),
    ('d_xbc', D_XBC),
    ('d_dt', D_HEADS),
    ('gates', N_BRANCH * D_MODEL),
)
IN_WIDTH = sum(size for _, size in IN_SEGMENTS)


def _split(x, sizes):
    out, off = [], 0
    for s in sizes:
        out.append(x[..., off:off + s])
        off += s
    return out

def layer_norm(x, g, b):
    xf = x.astype(jnp.float32)
    mu = jnp.mean(xf, axis=-1, keepdims=True)
    var = jnp.mean(jnp.square(xf - mu), axis=-1, keepdims=True)
    return ((xf - mu) * lax.rsqrt(var + LN_EPS) * g + b).astype(x.dtype)

def dilated_window_attention(qs, ks, vs):
    b, T = qs[0].shape[:2]
    scale = HEAD_DIM ** -0.5
    kps = [jnp.pad(k, ((0, 0), (w, 0), (0, 0), (0, 0))) for k, (w, _) in zip(ks, A_PATTERNS)]
    vps = [jnp.pad(v, ((0, 0), (w, 0), (0, 0), (0, 0))) for v, (w, _) in zip(vs, A_PATTERNS)]

    def block(i):
        start = i * Q_BLOCK
        outs, lses = [], []
        for q, kp, vp, (win, dil) in zip(qs, kps, vps, A_PATTERNS):
            nq, nk, span = Q_BLOCK // dil, win // dil, (win + Q_BLOCK) // dil
            qb = lax.dynamic_slice_in_dim(q, start, Q_BLOCK, axis=1).reshape(b, nq, dil, A_HEADS, HEAD_DIM)
            kb = lax.dynamic_slice_in_dim(kp, start, win + Q_BLOCK, axis=1).reshape(b, span, dil, A_HEADS, HEAD_DIM)
            vb = lax.dynamic_slice_in_dim(vp, start, win + Q_BLOCK, axis=1).reshape(b, span, dil, A_HEADS, HEAD_DIM)
            s = jnp.einsum('barhe,bcrhe->brhac', qb, kb).astype(jnp.float32) * scale
            a_idx = jnp.arange(nq)[:, None]
            c_idx = jnp.arange(span)[None, :]
            band = (c_idx >= a_idx) & (c_idx <= a_idx + nk)
            key_pos = start - win + jnp.arange(span)[None, :] * dil + jnp.arange(dil)[:, None]
            ok = band[None, :, :] & (key_pos >= 0)[:, None, :]
            s = jnp.where(ok[None, :, None], s, -jnp.inf)
            lse = jax.nn.logsumexp(s, axis=-1)
            p = jnp.exp(s - lse[..., None]).astype(vb.dtype)
            o = jnp.einsum('brhac,bcrhe->barhe', p, vb).reshape(b, Q_BLOCK, A_HEADS, HEAD_DIM)
            outs.append(o)
            lses.append(lse.transpose(0, 3, 1, 2).reshape(b, Q_BLOCK, A_HEADS))
        mix = jax.nn.softmax(jnp.stack(lses), axis=0)
        out = mix[0][..., None].astype(outs[0].dtype) * outs[0]
        for g in range(1, A_GROUPS):
            out = out + mix[g][..., None].astype(outs[g].dtype) * outs[g]
        return out

    out = lax.map(block, jnp.arange(T // Q_BLOCK))
    return out.transpose(1, 0, 2, 3, 4).reshape(b, T, A_WIDTH)

def indexer_sparse_attention(q, k, v, iq, ik, iw):
    b, T = q.shape[:2]
    top_k = min(TOPK_MAX, T // 4)
    scale = HEAD_DIM ** -0.5
    key_pos = jnp.arange(T)
    gather = jax.vmap(lambda arr, idx: arr[idx])

    def block(i):
        start = i * Q_BLOCK
        t = start + jnp.arange(Q_BLOCK)
        qi = lax.dynamic_slice_in_dim(iq, start, Q_BLOCK, axis=1)
        wi = lax.dynamic_slice_in_dim(iw, start, Q_BLOCK, axis=1).astype(jnp.float32)
        logits = jnp.einsum('bqhd,bsd->bqhs', qi, ik).astype(jnp.float32) * IDX_DIM ** -0.5
        score = jnp.einsum('bqhs,bqh->bqs', jax.nn.relu(logits), wi) * IDX_HEADS ** -0.5
        score = jnp.where((key_pos[None, :] <= t[:, None])[None], score, -jnp.inf)
        _, sel = lax.top_k(score, top_k)
        valid = sel <= t[None, :, None]
        kg = gather(k, sel)
        vg = gather(v, sel)
        qb = lax.dynamic_slice_in_dim(q, start, Q_BLOCK, axis=1)
        s = jnp.einsum('bqhe,bqjhe->bhqj', qb, kg).astype(jnp.float32) * scale
        s = jnp.where(valid[:, None], s, -jnp.inf)
        p = jax.nn.softmax(s, axis=-1).astype(vg.dtype)
        return jnp.einsum('bhqj,bqjhe->bqhe', p, vg)

    out = lax.map(block, jnp.arange(T // Q_BLOCK))
    return out.transpose(1, 0, 2, 3, 4).reshape(b, T, B_WIDTH)

def token_shift(x):
    return jnp.pad(x, ((0, 0), (1, 0), (0, 0)))[:, :-1]

def wkv7_scan(r, w, k, v, a, bb):
    b, T, H, N = r.shape

    def step(state, inp):
        rt, wt, kt, vt, at, bt = inp
        sa = jnp.einsum('bhij,bhj->bhi', state, at)
        state = state * wt[:, :, None, :] + sa[..., None] * bt[:, :, None, :] + vt[..., None] * kt[:, :, None, :]
        return state, jnp.einsum('bhij,bhj->bhi', state, rt)

    seq_major = tuple(jnp.moveaxis(t.astype(jnp.float32), 1, 0) for t in (r, w, k, v, a, bb))
    _, y = lax.scan(step, jnp.zeros((b, H, N, N), jnp.float32), seq_major)
    return jnp.moveaxis(y, 0, 1)

def rwkv7_time_mix(pc, mu, w0, w2, a0, a2, g2, k_k, k_a, r_k, gn_w, gn_b, v_first, v_lora):
    b, T, _ = pc.shape
    pc = pc + (token_shift(pc) - pc) * mu
    r, k, v, xw, xa, xg = _split(pc, (C_WIDTH, C_WIDTH, C_WIDTH, C_LORA_W, C_LORA_A, C_LORA_G))
    w = -jax.nn.softplus(-(w0 + jnp.tanh(xw) @ w2)) - 0.5
    a = jax.nn.sigmoid(a0 + xa @ a2)
    g = jax.nn.sigmoid(xg) @ g2
    if v_lora is not None:
        v0, v1, v2 = v_lora
        v = v + (v_first - v) * jax.nn.sigmoid(v0 + (v @ v1) @ v2)
    heads = lambda t: t.astype(jnp.float32).reshape(b, T, C_HEADS, HEAD_DIM)
    kk = heads(k * k_k)
    kk = kk / jnp.maximum(jnp.linalg.norm(kk, axis=-1, keepdims=True), 1e-12)
    k_mod = heads(k * (1.0 + (a - 1.0) * k_a))
    r_h, v_h, a_h = heads(r), heads(v), heads(a)
    decay = jnp.exp(-jnp.exp(heads(w)))
    y = wkv7_scan(r_h, decay, k_mod, v_h, -kk, kk * a_h)
    y_mu = jnp.mean(y, axis=-1, keepdims=True)
    y_var = jnp.mean(jnp.square(y - y_mu), axis=-1, keepdims=True)
    y = ((y - y_mu) * lax.rsqrt(y_var + C_GN_EPS)).reshape(b, T, C_WIDTH) * gn_w + gn_b
    bonus = jnp.sum(r_h * k_mod * r_k, axis=-1, keepdims=True) * v_h
    o = (y + bonus.reshape(b, T, C_WIDTH)) * g
    return o.astype(pc.dtype), v

def ssd_chunked(x, a, bm, cm):
    b, T, H, P = x.shape
    nc = T // D_CHUNK
    x = x.reshape(b, nc, D_CHUNK, H, P)
    bm = bm.reshape(b, nc, D_CHUNK, H, -1)
    cm = cm.reshape(b, nc, D_CHUNK, H, -1)
    a_cs = jnp.cumsum(a.reshape(b, nc, D_CHUNK, H).transpose(0, 3, 1, 2), axis=-1)
    seg = a_cs[..., :, None] - a_cs[..., None, :]
    causal = jnp.tril(jnp.ones((D_CHUNK, D_CHUNK), dtype=bool))
    decay_ls = jnp.exp(jnp.where(causal, seg, -jnp.inf))
    scores = jnp.einsum('bclhn,bcshn->bhcls', cm, bm) * decay_ls
    y_diag = jnp.einsum('bhcls,bcshp->bclhp', scores, x)
    decay_to_end = jnp.exp(a_cs[..., -1:] - a_cs)
    chunk_states = jnp.einsum('bclhn,bhcl,bclhp->bchpn', bm, decay_to_end, x)
    chunk_decay = jnp.exp(a_cs[..., -1])

    def step(state, inp):
        st, dc = inp
        return state * dc[..., None, None] + st, state

    _, states_in = lax.scan(step, jnp.zeros((b, H, P, bm.shape[-1]), jnp.float32),
                            (jnp.moveaxis(chunk_states, 1, 0), jnp.moveaxis(chunk_decay, 2, 0)))
    states_in = jnp.moveaxis(states_in, 0, 1)
    y_off = jnp.einsum('bclhn,bchpn,bhcl->bclhp', cm, states_in, jnp.exp(a_cs))
    return (y_diag + y_off).reshape(b, T, H, P)

def mamba2_mixer(z, xbc, dt_raw, conv_w, conv_b, dt_bias, a_log, d_skip, norm_w):
    b, T, _ = z.shape
    xbc = lax.conv_general_dilated(xbc, conv_w[:, None, :], window_strides=(1,),
                                   padding=[(D_CONV - 1, 0)],
                                   dimension_numbers=('NWC', 'WIO', 'NWC'),
                                   feature_group_count=D_XBC)
    xbc = jax.nn.silu(xbc + conv_b).astype(jnp.float32)
    heads_per_group = D_HEADS // D_GROUPS
    xs = xbc[..., :D_INNER].reshape(b, T, D_HEADS, HEAD_DIM)
    bm = xbc[..., D_INNER:D_INNER + D_GROUPS * D_STATE].reshape(b, T, D_GROUPS, D_STATE)
    cm = xbc[..., D_INNER + D_GROUPS * D_STATE:].reshape(b, T, D_GROUPS, D_STATE)
    bm = jnp.repeat(bm, heads_per_group, axis=2)
    cm = jnp.repeat(cm, heads_per_group, axis=2)
    dt = jax.nn.softplus(dt_raw.astype(jnp.float32) + dt_bias.astype(jnp.float32))
    a = -jnp.exp(a_log.astype(jnp.float32))
    y = ssd_chunked(xs * dt[..., None], dt * a, bm, cm) + d_skip.astype(jnp.float32)[:, None] * xs
    y = y.reshape(b, T, D_INNER) * jax.nn.silu(z.astype(jnp.float32))
    y = y.reshape(b, T, D_GROUPS, D_INNER // D_GROUPS)
    y = y * lax.rsqrt(jnp.mean(jnp.square(y), axis=-1, keepdims=True) + D_NORM_EPS)
    return (y.reshape(b, T, D_INNER) * norm_w).astype(z.dtype)

def grouped_expert_ffn(x2d, expert, gate, w_gate, w_up, w_down):
    m, dm = x2d.shape
    n_assign = m * TOP_K_EXPERTS
    flat_e = expert.reshape(-1)
    flat_tok = jnp.arange(n_assign) // TOP_K_EXPERTS
    flat_gate = gate.reshape(-1)
    order = jnp.argsort(flat_e)
    se, stok, sgate = flat_e[order], flat_tok[order], flat_gate[order]
    counts = jnp.bincount(flat_e, length=N_EXPERTS)
    padded = (counts + MOE_BLOCK - 1) // MOE_BLOCK * MOE_BLOCK
    pad_end = jnp.cumsum(padded)
    pad_start = pad_end - padded
    start = jnp.cumsum(counts) - counts
    dest = pad_start[se] + jnp.arange(n_assign) - start[se]
    cap = (n_assign + N_EXPERTS * (MOE_BLOCK - 1) + MOE_BLOCK - 1) // MOE_BLOCK * MOE_BLOCK
    n_blocks = cap // MOE_BLOCK
    buf_tok = jnp.full((cap,), m, dtype=jnp.int32).at[dest].set(stok)
    x_ext = jnp.concatenate([x2d, jnp.zeros((1, dm), x2d.dtype)], axis=0)
    xb = x_ext[buf_tok].reshape(n_blocks, MOE_BLOCK, dm)
    blk_expert = jnp.minimum(jnp.searchsorted(pad_end, jnp.arange(n_blocks) * MOE_BLOCK, side='right'),
                             N_EXPERTS - 1)

    def expert_block(args):
        xblk, e = args
        h = jax.nn.silu(xblk @ w_gate[e]) * (xblk @ w_up[e])
        return h @ w_down[e]

    yb = lax.map(expert_block, (xb, blk_expert)).reshape(cap, dm)
    y = yb[dest] * sgate[:, None]
    return jnp.zeros_like(x2d).at[stok].add(y)

def hierarchical_moe(x2d, wg, bg, we, be, w_gate, w_up, w_down):
    m = x2d.shape[0]
    xf = x2d.astype(jnp.float32)
    p_group = jax.nn.softmax(xf @ wg.astype(jnp.float32) + bg.astype(jnp.float32), axis=-1)
    pg_top, g_sel = lax.top_k(p_group, 1)
    logits_e = (xf @ we.astype(jnp.float32) + be.astype(jnp.float32)).reshape(m, N_EXPERT_GROUPS, EXPERTS_PER_GROUP)
    logits_e = logits_e[jnp.arange(m), g_sel[:, 0]]
    pe_top, e_sel = lax.top_k(jax.nn.softmax(logits_e, axis=-1), TOP_K_EXPERTS)
    gate = pg_top * pe_top / jnp.sum(pe_top, axis=-1, keepdims=True)
    expert = g_sel * EXPERTS_PER_GROUP + e_sel
    return grouped_expert_ffn(x2d, expert, gate.astype(x2d.dtype), w_gate, w_up, w_down)

def first_inputs(seed: int = 0) -> dict:
    key = jax.random.key(seed)
    ks = iter(jax.random.split(key, 48))
    L = DEPTH

    def nrm(shape, scale):
        return jax.random.normal(next(ks), shape, jnp.float32) * scale

    def unif(shape, lo, hi):
        return jax.random.uniform(next(ks), shape, jnp.float32, minval=lo, maxval=hi)

    dt = jnp.exp(unif((L, D_HEADS), math.log(1e-3), math.log(1e-1)))
    return {
        'x': nrm((BATCH, SEQ, D_MODEL), 1.0),
        'w_in': nrm((L, D_MODEL, IN_WIDTH), D_MODEL ** -0.5),
        'c_mu': unif((L, C_IN), 0.0, 1.0),
        'c_w0': unif((L, C_WIDTH), -6.0, -1.0),
        'c_w2': nrm((L, C_LORA_W, C_WIDTH), 0.1),
        'c_a0': nrm((L, C_WIDTH), 0.1),
        'c_a2': nrm((L, C_LORA_A, C_WIDTH), C_LORA_A ** -0.5),
        'c_g2': nrm((L, C_LORA_G, C_WIDTH), C_LORA_G ** -0.5),
        'c_kk': 0.85 + nrm((L, C_WIDTH), 0.02),
        'c_ka': 1.0 + nrm((L, C_WIDTH), 0.02),
        'c_rk': nrm((L, C_HEADS, HEAD_DIM), 0.1),
        'c_gn_w': 1.0 + nrm((L, C_WIDTH), 0.02),
        'c_gn_b': nrm((L, C_WIDTH), 0.02),
        'c_v0': nrm((L - 1, C_WIDTH), 0.1),
        'c_v1': nrm((L - 1, C_WIDTH, C_LORA_V), C_WIDTH ** -0.5),
        'c_v2': nrm((L - 1, C_LORA_V, C_WIDTH), C_LORA_V ** -0.5),
        'd_conv_w': nrm((L, D_CONV, D_XBC), D_CONV ** -0.5),
        'd_conv_b': nrm((L, D_XBC), 0.02),
        'd_dt_bias': dt + jnp.log(-jnp.expm1(-dt)),
        'd_a_log': jnp.log(unif((L, D_HEADS), 1.0, 16.0)),
        'd_skip': 1.0 + nrm((L, D_HEADS), 0.02),
        'd_norm_w': 1.0 + nrm((L, D_INNER), 0.02),
        'w_branch': nrm((L, N_BRANCH, BRANCH_WIDTH, D_MODEL), BRANCH_WIDTH ** -0.5),
        'w_out': nrm((L, D_MODEL, D_MODEL), D_MODEL ** -0.5 * DEEPNORM_BETA),
        'ln1_g': 1.0 + nrm((L, D_MODEL), 0.02),
        'ln1_b': nrm((L, D_MODEL), 0.02),
        'r_group': nrm((L, D_MODEL, N_EXPERT_GROUPS), D_MODEL ** -0.5),
        'r_group_b': nrm((L, N_EXPERT_GROUPS), 0.01),
        'r_expert': nrm((L, D_MODEL, N_EXPERTS), D_MODEL ** -0.5),
        'r_expert_b': nrm((L, N_EXPERTS), 0.01),
        'e_gate': nrm((L, N_EXPERTS, D_MODEL, D_EXPERT), D_MODEL ** -0.5),
        'e_up': nrm((L, N_EXPERTS, D_MODEL, D_EXPERT), D_MODEL ** -0.5),
        'e_down': nrm((L, N_EXPERTS, D_EXPERT, D_MODEL), D_EXPERT ** -0.5 * DEEPNORM_BETA),
        'ln2_g': 1.0 + nrm((L, D_MODEL), 0.02),
        'ln2_b': nrm((L, D_MODEL), 0.02),
    }

def first_block(x, w_in, c_mu, c_w0, c_w2, c_a0, c_a2, c_g2, c_kk, c_ka, c_rk, c_gn_w, c_gn_b,
              c_v0, c_v1, c_v2, d_conv_w, d_conv_b, d_dt_bias, d_a_log, d_skip, d_norm_w,
              w_branch, w_out, ln1_g, ln1_b, r_group, r_group_b, r_expert, r_expert_b,
              e_gate, e_up, e_down, ln2_g, ln2_b):
    b, T, _ = x.shape
    v_first = None
    for l in range(DEPTH):
        seg, off = {}, 0
        for name, size in IN_SEGMENTS:
            seg[name] = x @ w_in[l, :, off:off + size]
            off += size

        a_qkv = seg['a_qkv'].reshape(b, T, 3, A_GROUPS, A_HEADS, HEAD_DIM)
        o_a = dilated_window_attention([a_qkv[:, :, 0, g] for g in range(A_GROUPS)],
                                       [a_qkv[:, :, 1, g] for g in range(A_GROUPS)],
                                       [a_qkv[:, :, 2, g] for g in range(A_GROUPS)])

        b_qkv = seg['b_qkv'].reshape(b, T, 3, B_HEADS, HEAD_DIM)
        o_b = indexer_sparse_attention(b_qkv[:, :, 0], b_qkv[:, :, 1], b_qkv[:, :, 2],
                                       seg['b_idx_q'].reshape(b, T, IDX_HEADS, IDX_DIM),
                                       seg['b_idx_k'], seg['b_idx_w'])

        v_lora = None if l == 0 else (c_v0[l - 1], c_v1[l - 1], c_v2[l - 1])
        o_c, v_c = rwkv7_time_mix(seg['c_in'], c_mu[l], c_w0[l], c_w2[l], c_a0[l], c_a2[l], c_g2[l],
                                  c_kk[l], c_ka[l], c_rk[l], c_gn_w[l], c_gn_b[l], v_first, v_lora)
        if l == 0:
            v_first = v_c

        o_d = mamba2_mixer(seg['d_z'], seg['d_xbc'], seg['d_dt'], d_conv_w[l], d_conv_b[l],
                           d_dt_bias[l], d_a_log[l], d_skip[l], d_norm_w[l])

        gates = jax.nn.sigmoid(seg['gates'].reshape(b, T, N_BRANCH, D_MODEL))
        merged = jnp.zeros_like(x)
        for n, o_n in enumerate((o_a, o_b, o_c, o_d)):
            merged = merged + gates[:, :, n] * (o_n @ w_branch[l, n])
        x = layer_norm(DEEPNORM_ALPHA * x + merged @ w_out[l], ln1_g[l], ln1_b[l])

        y = hierarchical_moe(x.reshape(b * T, D_MODEL), r_group[l], r_group_b[l], r_expert[l],
                             r_expert_b[l], e_gate[l], e_up[l], e_down[l])
        x = layer_norm(DEEPNORM_ALPHA * x + y.reshape(b, T, D_MODEL), ln2_g[l], ln2_b[l])
    return x


_first_inputs = first_inputs


def first_inputs(seed=0):
    import zlib

    import numpy as np

    out = dict(_first_inputs(seed))
    spreads = {}
    factors = {'c_w2': 8.0,
     'c_a0': 5.463,
     'c_kk': 200.0,
     'c_ka': 63.395,
     'c_gn_w': 127.014,
     'c_gn_b': 106.223,
     'd_conv_b': 6.56,
     'd_a_log': 24.448,
     'd_skip': 200.0,
     'd_norm_w': 67.453,
     'r_group_b': 18.981,
     'r_expert_b': 18.673,
     'ln2_g': 22.895,
     'ln2_b': 22.986,
     'd_dt_bias': 27.36}
    for name, (base, spread) in spreads.items():
        noise = np.random.default_rng([zlib.crc32(name.encode()), seed]).standard_normal(out[name].shape)
        drawn = base * np.exp(spread * noise) if base else spread * noise
        out[name] = jnp.asarray(drawn.astype(out[name].dtype))
    for name, factor in factors.items():
        out[name] = (out[name] * factor).astype(out[name].dtype)
    return out


_narrow_inputs = first_inputs


def first_inputs(seed=0):

    out = dict(_narrow_inputs(seed))
    wider = {'c_kk': 5.83,
     'c_ka': 3.1,
     'c_gn_w': 3.73,
     'c_gn_b': 4.2,
     'd_skip': 12.0,
     'd_norm_w': 3.54,
     'ln2_g': 3.2,
     'ln2_b': 3.2}
    for name, times in wider.items():
        mean = out[name].mean()
        out[name] = (mean + times * (out[name] - mean)).astype(out[name].dtype)
    return out


DEPTH_2 = 2

CTX_LEN = 256
GRID_W = 64
MLA_HEADS = 8
MLA_NOPE = 64
MLA_ROPE = 32
MLA_V = 64
MLA_QK = MLA_NOPE + MLA_ROPE
Q_LORA = 768
KV_LORA = 256
NA_HEADS = 8
NA_DIM = 64
NA_KH = 8
NA_KW = 16
D_FF = 4 * D_MODEL
N_BRANCH_2 = 2
ROPE_BASE = 10000.0
ROPE_PAIRS = MLA_ROPE // 4
EPS = 1e-6
OFF_CQ = N_BRANCH_2 * D_MODEL
OFF_CKV = OFF_CQ + Q_LORA
OFF_KR = OFF_CKV + KV_LORA
OFF_NA = OFF_KR + MLA_ROPE
IN_COLS = OFF_NA + 3 * NA_HEADS * NA_DIM


def rms_norm(x, g):
    xf = x.astype(jnp.float32)
    y = xf * lax.rsqrt(jnp.mean(xf * xf, axis=-1, keepdims=True) + EPS)
    return (y * g.astype(jnp.float32)).astype(x.dtype)

def modulate(h, shift, scale):
    return h * (1 + scale) + shift

def rope_half(x, ang):
    m = x.shape[-1] // 2
    x1, x2 = x[..., :m], x[..., m:]
    cos = jnp.cos(ang).astype(x.dtype)
    sin = jnp.sin(ang).astype(x.dtype)
    return jnp.concatenate([x1 * cos - x2 * sin, x1 * sin + x2 * cos], axis=-1)

def rope_2d(x, ang_r, ang_c):
    half = x.shape[-1] // 2
    return jnp.concatenate([rope_half(x[..., :half], ang_r), rope_half(x[..., half:], ang_c)], axis=-1)

def mixer_proj(h, w_in, g_qa, w_uq, g_kva, w_ukv, g_mq, g_mk, g_nq, g_nk):
    b_, s_ = h.shape[0], h.shape[1]
    p = h @ w_in
    gate_logits = p[..., :OFF_CQ]
    c_q = p[..., OFF_CQ:OFF_CKV]
    c_kv = p[..., OFF_CKV:OFF_KR]
    k_r = p[..., OFF_KR:OFF_NA]
    na = p[..., OFF_NA:].reshape(b_, s_, 3, NA_HEADS, NA_DIM)
    mq = (rms_norm(c_q, g_qa) @ w_uq).reshape(b_, s_, MLA_HEADS, MLA_QK)
    kv = (rms_norm(c_kv, g_kva) @ w_ukv).reshape(b_, s_, MLA_HEADS, MLA_NOPE + MLA_V)
    k_nope, mv = kv[..., :MLA_NOPE], kv[..., MLA_NOPE:]
    k_rope = jnp.broadcast_to(k_r[:, :, None, :], (b_, s_, MLA_HEADS, MLA_ROPE))
    mk = jnp.concatenate([k_nope, k_rope], axis=-1)
    mq = rms_norm(mq, g_mq)
    mk = rms_norm(mk, g_mk)
    nq = rms_norm(na[:, :, 0], g_nq)
    nk = rms_norm(na[:, :, 1], g_nk)
    nv = na[:, :, 2]
    return gate_logits, mq, mk, mv, nq, nk, nv

def dense_attention(q, k, v):
    scale = 1.0 / math.sqrt(q.shape[-1])
    s = jnp.einsum("bqhd,bkhd->bhqk", q, k).astype(jnp.float32) * scale
    p = jax.nn.softmax(s, axis=-1).astype(v.dtype)
    return jnp.einsum("bhqk,bkhe->bqhe", p, v)

def blocked_attention(q, k, v):
    b_, s_, h_, d_ = q.shape
    nb = s_ // Q_BLOCK
    qb = jnp.moveaxis(q.reshape(b_, nb, Q_BLOCK, h_, d_), 1, 0)
    ob = lax.map(lambda blk: dense_attention(blk, k, v), qb)
    return jnp.moveaxis(ob, 0, 1).reshape(b_, s_, h_, v.shape[-1])

def neighborhood_attention(q, k, v, k_ctx, v_ctx, rpb):
    b_, s_, h_, d_ = q.shape
    rows = s_ // GRID_W
    kh = min(NA_KH, rows)
    kw = NA_KW
    scale = 1.0 / math.sqrt(d_)
    to_grid = lambda t: t.reshape(b_, rows, GRID_W, h_, d_).transpose(1, 0, 3, 2, 4)
    q_g, k_g, v_g = to_grid(q), to_grid(k), to_grid(v)
    cols = jnp.arange(GRID_W)
    c_start = jnp.clip(cols - kw // 2, 0, GRID_W - kw)
    col_idx = c_start[:, None] + jnp.arange(kw)[None, :]
    dc_idx = col_idx - cols[:, None] + (NA_KW - 1)
    rpb_cols = rpb[:, :, dc_idx]

    def row_fn(args):
        q_r, r = args
        r_start = jnp.clip(r - kh // 2, 0, rows - kh)
        k_rows = lax.dynamic_slice_in_dim(k_g, r_start, kh, axis=0)
        v_rows = lax.dynamic_slice_in_dim(v_g, r_start, kh, axis=0)
        k_win = k_rows[:, :, :, col_idx]
        v_win = v_rows[:, :, :, col_idx]
        dr_idx = r_start + jnp.arange(kh) - r + (NA_KH - 1)
        bias = jnp.transpose(jnp.take(rpb_cols, dr_idx, axis=1), (0, 2, 1, 3))
        s_win = jnp.einsum("bhqd,ibhqjd->bhqij", q_r, k_win).astype(jnp.float32) * scale
        s_win = (s_win + bias.astype(jnp.float32)).reshape(b_, h_, GRID_W, kh * kw)
        s_ctx = jnp.einsum("bhqd,bkhd->bhqk", q_r, k_ctx).astype(jnp.float32) * scale
        p = jax.nn.softmax(jnp.concatenate([s_win, s_ctx], axis=-1), axis=-1).astype(v.dtype)
        p_win = p[..., :kh * kw].reshape(b_, h_, GRID_W, kh, kw)
        p_ctx = p[..., kh * kw:]
        return (jnp.einsum("bhqij,ibhqjd->bhqd", p_win, v_win)
                + jnp.einsum("bhqk,bkhd->bhqd", p_ctx, v_ctx))

    o = lax.map(row_fn, (q_g, jnp.arange(rows)))
    return o.transpose(1, 0, 3, 2, 4).reshape(b_, s_, h_ * d_)

def gated_merge(gate_logits, y_mla, y_na, w_mla_o, w_na_o, w_out):
    g = jax.nn.sigmoid(gate_logits.astype(jnp.float32)).astype(y_mla.dtype)
    y = g[..., :D_MODEL] * (y_mla @ w_mla_o) + g[..., D_MODEL:] * (y_na @ w_na_o)
    return y @ w_out

def squared_relu_mlp(h, w_ff1, w_ff2):
    return jnp.square(jax.nn.relu(h @ w_ff1)) @ w_ff2

def _normal(key, shape, scale):
    return jax.random.normal(key, shape, jnp.float32) * scale

def second_inputs(seed: int = 0) -> dict:
    key = jax.random.key(seed)
    ks = jax.random.split(key, 24)
    L = DEPTH_2
    gain = lambda k, n: 1.0 + _normal(k, (L, n), 0.1)
    return {
        "x": _normal(ks[0], (BATCH, SEQ, D_MODEL), 1.0),
        "c": _normal(ks[1], (BATCH, D_MODEL), 1.0),
        "ctx": _normal(ks[2], (BATCH, CTX_LEN, D_MODEL), 1.0),
        "c_ctx": _normal(ks[3], (D_MODEL,), 1.0),
        "w_ada": _normal(ks[4], (L, D_MODEL, 6 * D_MODEL), D_MODEL ** -0.5),
        "b_ada": _normal(ks[5], (L, 6 * D_MODEL), 0.02),
        "g_attn": gain(ks[6], D_MODEL),
        "w_in": _normal(ks[7], (L, D_MODEL, IN_COLS), D_MODEL ** -0.5),
        "g_qa": gain(ks[8], Q_LORA),
        "w_uq": _normal(ks[9], (L, Q_LORA, MLA_HEADS * MLA_QK), Q_LORA ** -0.5),
        "g_kva": gain(ks[10], KV_LORA),
        "w_ukv": _normal(ks[11], (L, KV_LORA, MLA_HEADS * (MLA_NOPE + MLA_V)), KV_LORA ** -0.5),
        "g_mla_q": gain(ks[12], MLA_QK),
        "g_mla_k": gain(ks[13], MLA_QK),
        "g_na_q": gain(ks[14], NA_DIM),
        "g_na_k": gain(ks[15], NA_DIM),
        "rpb": _normal(ks[16], (L, NA_HEADS, 2 * NA_KH - 1, 2 * NA_KW - 1), 0.1),
        "w_mla_o": _normal(ks[17], (L, MLA_HEADS * MLA_V, D_MODEL), (MLA_HEADS * MLA_V) ** -0.5),
        "w_na_o": _normal(ks[18], (L, NA_HEADS * NA_DIM, D_MODEL), (NA_HEADS * NA_DIM) ** -0.5),
        "w_out": _normal(ks[19], (L, D_MODEL, D_MODEL), D_MODEL ** -0.5),
        "g_mlp": gain(ks[20], D_MODEL),
        "w_ff1": _normal(ks[21], (L, D_MODEL, D_FF), D_MODEL ** -0.5),
        "w_ff2": _normal(ks[22], (L, D_FF, D_MODEL), D_FF ** -0.5),
    }

def second_block(x, c, ctx, c_ctx, w_ada, b_ada, g_attn, w_in, g_qa, w_uq, g_kva, w_ukv,
              g_mla_q, g_mla_k, g_na_q, g_na_k, rpb, w_mla_o, w_na_o, w_out,
              g_mlp, w_ff1, w_ff2):
    b_, s_, _ = x.shape
    l_ = ctx.shape[1]
    t = jnp.arange(s_)
    inv_freq = ROPE_BASE ** (-jnp.arange(ROPE_PAIRS, dtype=jnp.float32) / ROPE_PAIRS)
    ang_r = ((t // GRID_W).astype(jnp.float32)[:, None] * inv_freq)[:, None, :]
    ang_c = ((t % GRID_W).astype(jnp.float32)[:, None] * inv_freq)[:, None, :]
    silu_c = jax.nn.silu(c)
    silu_ctx = jax.nn.silu(c_ctx)
    x_lat, x_ctx = x, ctx
    for l in range(DEPTH_2):
        last = l == DEPTH_2 - 1
        mod_lat = (silu_c @ w_ada[l] + b_ada[l])[:, None, :]
        mod_ctx = silu_ctx @ w_ada[l] + b_ada[l]
        sh1, sc1, gt1, sh2, sc2, gt2 = jnp.split(mod_lat, 6, axis=-1)
        csh1, csc1, cgt1, csh2, csc2, cgt2 = jnp.split(mod_ctx, 6, axis=-1)
        proj_w = (w_in[l], g_qa[l], w_uq[l], g_kva[l], w_ukv[l],
                  g_mla_q[l], g_mla_k[l], g_na_q[l], g_na_k[l])

        h_c = modulate(rms_norm(x_ctx, g_attn[l]), csh1, csc1)
        gl_c, mq_c, mk_c, mv_c, nq_c, nk_c, nv_c = mixer_proj(h_c, *proj_w)

        h = modulate(rms_norm(x_lat, g_attn[l]), sh1, sc1)
        gl, mq, mk, mv, nq, nk, nv = mixer_proj(h, *proj_w)
        mq = jnp.concatenate([mq[..., :MLA_NOPE], rope_2d(mq[..., MLA_NOPE:], ang_r, ang_c)], axis=-1)
        mk = jnp.concatenate([mk[..., :MLA_NOPE], rope_2d(mk[..., MLA_NOPE:], ang_r, ang_c)], axis=-1)
        y_mla = blocked_attention(mq, jnp.concatenate([mk_c, mk], axis=1),
                                  jnp.concatenate([mv_c, mv], axis=1)).reshape(b_, s_, MLA_HEADS * MLA_V)
        y_na = neighborhood_attention(nq, nk, nv, nk_c, nv_c, rpb[l])
        x_lat = x_lat + gt1 * gated_merge(gl, y_mla, y_na, w_mla_o[l], w_na_o[l], w_out[l])

        if not last:
            y_mla_c = dense_attention(mq_c, mk_c, mv_c).reshape(b_, l_, MLA_HEADS * MLA_V)
            y_na_c = dense_attention(nq_c, nk_c, nv_c).reshape(b_, l_, NA_HEADS * NA_DIM)
            x_ctx = x_ctx + cgt1 * gated_merge(gl_c, y_mla_c, y_na_c, w_mla_o[l], w_na_o[l], w_out[l])
            h2_c = modulate(rms_norm(x_ctx, g_mlp[l]), csh2, csc2)
            x_ctx = x_ctx + cgt2 * squared_relu_mlp(h2_c, w_ff1[l], w_ff2[l])

        h2 = modulate(rms_norm(x_lat, g_mlp[l]), sh2, sc2)
        x_lat = x_lat + gt2 * squared_relu_mlp(h2, w_ff1[l], w_ff2[l])
    return x_lat


def setup_inputs(seed=0):
    out = dict(first_inputs(seed))
    for name, value in second_inputs(seed + 1).items():
        if name != "x":
            out[name + "_2"] = value
    return out


def reference(
    x, w_in, c_mu, c_w0, c_w2, c_a0, c_a2, c_g2, c_kk, c_ka, c_rk, c_gn_w, c_gn_b, c_v0, c_v1,
    c_v2, d_conv_w, d_conv_b, d_dt_bias, d_a_log, d_skip, d_norm_w, w_branch, w_out, ln1_g,
    ln1_b, r_group, r_group_b, r_expert, r_expert_b, e_gate, e_up, e_down, ln2_g, ln2_b, c_2,
    ctx_2, c_ctx_2, w_ada_2, b_ada_2, g_attn_2, w_in_2, g_qa_2, w_uq_2, g_kva_2, w_ukv_2,
    g_mla_q_2, g_mla_k_2, g_na_q_2, g_na_k_2, rpb_2, w_mla_o_2, w_na_o_2, w_out_2, g_mlp_2,
    w_ff1_2, w_ff2_2,
):
    x = first_block(
        x, w_in, c_mu, c_w0, c_w2, c_a0, c_a2, c_g2, c_kk, c_ka, c_rk, c_gn_w, c_gn_b, c_v0,
        c_v1, c_v2, d_conv_w, d_conv_b, d_dt_bias, d_a_log, d_skip, d_norm_w, w_branch, w_out,
        ln1_g, ln1_b, r_group, r_group_b, r_expert, r_expert_b, e_gate, e_up, e_down, ln2_g,
        ln2_b,
    )
    return second_block(
        x, c_2, ctx_2, c_ctx_2, w_ada_2, b_ada_2, g_attn_2, w_in_2, g_qa_2, w_uq_2, g_kva_2,
        w_ukv_2, g_mla_q_2, g_mla_k_2, g_na_q_2, g_na_k_2, rpb_2, w_mla_o_2, w_na_o_2, w_out_2,
        g_mlp_2, w_ff1_2, w_ff2_2,
    )


_drawn_inputs = setup_inputs


def setup_inputs(seed=0):
    import zlib

    import numpy as np

    out = dict(_drawn_inputs(seed))
    spreads = {}
    factors = {'ctx_2': 8.0,
     'c_ctx_2': 5.579,
     'b_ada_2': 8.0,
     'g_attn_2': 8.0,
     'w_in_2': 3.884,
     'g_qa_2': 8.0,
     'w_uq_2': 8.0,
     'g_kva_2': 8.0,
     'w_ukv_2': 6.491,
     'g_mla_q_2': 8.0,
     'g_mla_k_2': 8.0,
     'g_na_q_2': 8.0,
     'g_na_k_2': 8.0,
     'rpb_2': 8.0,
     'w_mla_o_2': 6.539,
     'w_na_o_2': 4.628,
     'w_out_2': 3.965,
     'g_mlp_2': 6.758}
    for name, (base, spread) in spreads.items():
        noise = np.random.default_rng([zlib.crc32(name.encode()), seed]).standard_normal(out[name].shape)
        drawn = base * np.exp(spread * noise) if base else spread * noise
        out[name] = jnp.asarray(drawn.astype(out[name].dtype))
    for name, factor in factors.items():
        out[name] = (out[name] * factor).astype(out[name].dtype)
    return out
```

```python
from contextlib import ExitStack

import concourse.bass as bass
from concourse import mybir

F32 = mybir.dt.float32
I32 = mybir.dt.int32
U32 = mybir.dt.uint32
ALU = mybir.AluOpType
ACT = mybir.ActivationFunctionType
AX = mybir.AxisListType.X

P = 128
BANK = 512
BANKS = 8
T = 512
TT = T // P
D = 1024
DK = D // P
HD = 64
RING = 4
TILE = DK * BANK
NEG = -1.0e30

A_G, A_H = 3, 4
A_W = A_H * HD
OFF_A = 0
OFF_B = OFF_A + 3 * A_G * A_W
B_W = 256
OFF_IQ = OFF_B + 3 * B_W
OFF_IK = OFF_IQ + 256
OFF_IW = OFF_IK + 64
OFF_C = OFF_IW + 4
C_W = 256
C_IN = 896
OFF_DZ = OFF_C + C_IN
OFF_XBC = OFF_DZ + 256
OFF_DT = OFF_XBC + 512
OFF_GATES = OFF_DT + 4
TOPK = 128
LN_EPS = 1e-5
ALPHA = 2.0 ** 0.25


class Machine:

    def __init__(self, nc, A, out):
        self.nc, self.A, self.out, self.groups = nc, A, out, 0


class Layer:

    def __init__(self, tq):
        self.tq = tq


class Route:

    def __init__(self, dest, gate, expert):
        self.dest, self.gate, self.expert = dest, gate, expert


class Unit:

    def __init__(self, segs, pv, out):
        self.segs, self.pv, self.out = segs, pv, out


class Group:

    def __init__(self, pe, evac, on, tile, after_v, after_s):
        self.pe, self.evac, self.on, self.tile = pe, evac, on, tile
        self.after_v, self.after_s = after_v, after_s


def on_scalar(eng):
    return isinstance(eng, bass.BassScalarEngine)


class Signals:

    def __init__(self, nc, stage):
        self._nc, self._stage, self._made = nc, stage, {}

    def __getitem__(self, name):
        if name not in self._made:
            self._made[name] = self._nc.alloc_semaphore(name=f"{self._stage}_{name}")
        return self._made[name]

    def close(self):
        if self._made:
            self._nc.clear_and_free_semaphores(list(self._made.values()))
            self._nc.all_engine_barrier()


class Chain:

    def __init__(self, eng, sem):
        self.eng, self.sem, self.n = eng, sem, 0

    def __call__(self, ins):
        self.n += 1
        ins.then_inc(self.sem, 1)
        self.eng.wait_ge(self.sem, self.n)

    def post(self, ins):
        self.n += 1
        ins.then_inc(self.sem, 1)


class Stage:

    def __init__(self, nc, name):
        self.nc, self.name = nc, name

    def __enter__(self):
        self.ctx = ExitStack()
        self.sig = Signals(self.nc, self.name)
        return self

    def sb(self, name, shape, dt=F32):
        return self.ctx.enter_context(self.nc.sbuf_tensor(f"{self.name}_{name}", shape, dt))

    def __exit__(self, *e):
        if e[0] is None:
            self.sig.close()
        self.ctx.close()


class Weights:

    def __init__(self, nc, ring, tiles, groups_done):
        self.ring, self.tiles, self.groups_done = ring, tiles, groups_done
        self.landed = [nc.alloc_semaphore(name=f"weights_landed{s}") for s in range(RING)]
        self.issued, self.taken = 0, 0
        self.last_group = {}

    def view(self, i):
        _, k, n = self.tiles[i]
        return self.ring[:, i % RING, 0:k * n].rearrange("p (k n) -> p k n", k=k)

    def load(self, sp, upto):
        while self.issued < min(upto, len(self.tiles)):
            i = self.issued
            if i >= RING:
                sp.wait_ge(self.groups_done, self.last_group[i - RING])
            sp.dma_start(self.view(i), self.tiles[i][0]).then_inc(self.landed[i % RING], 16)
            self.issued += 1

    def arrived(self, pe, i):
        pe.wait_ge(self.landed[i % RING], 16 * (i // RING + 1))


def weight_tiles(w, c0, c1, width=BANK):
    k = w.shape[0] // P
    return [(w[:, c:min(c + width, c1)].rearrange("(k p) n -> p k n", p=P), k, min(width, c1 - c))
            for c in range(c0, c1, width)]


def group(pe, evac, on, tile=None, after_v=0, after_s=0):
    return Group(pe, evac, on, tile, after_v, after_s)


def products(M, name, groups, tiles=0, banks=range(BANKS), extra=None):
    nc, W = M.nc, M.weights
    sig, base, nb = Signals(nc, name), M.groups, len(banks)
    at = {"v": [], "s": []}
    for i, g in enumerate(groups):
        at[g.on].append(i)
        if g.tile is not None:
            W.last_group[g.tile] = base + i + 1
    count = [at[g.on].index(i) + 1 for i, g in enumerate(groups)]
    moved = {"v": sig["moved_v"], "s": sig["moved_s"]}
    W.taken += tiles
    M.groups += len(groups)

    with nc.Block() as block:
        @block.sync
        def _(sp):
            if extra and "sync" in extra:
                extra["sync"](sp)
            W.load(sp, W.taken + RING)

        if extra and "gpsimd" in extra:
            block.gpsimd(extra["gpsimd"])

        @block.tensor
        def _(pe):
            seen = -1
            for i, g in enumerate(groups):
                if g.tile is not None and g.tile > seen:
                    W.arrived(pe, g.tile)
                    seen = g.tile
                if i >= nb:
                    pe.wait_ge(moved[groups[i - nb].on], count[i - nb])
                g.pe(pe, M.ps[:, banks[i % nb], :]).then_inc(W.groups_done, 1)

        def mover(eng, on):
            link = Chain(eng, sig["chain_" + on])
            for i in at[on]:
                g = groups[i]
                eng.wait_ge(W.groups_done, base + i + 1)
                if g.after_v:
                    eng.wait_ge(moved["v"], g.after_v)
                if g.after_s:
                    eng.wait_ge(moved["s"], g.after_s)
                g.evac(eng, M.ps[:, banks[i % nb], :], link).then_inc(moved[on], 1)

        @block.vector
        def _(dve):
            mover(dve, "v")

        @block.scalar
        def _(act):
            mover(act, "s")
    sig.close()


def move(eng, out, in_, scale=None):
    if on_scalar(eng):
        return eng.activation(out, in_, ACT.Copy, scale=1.0 if scale is None else scale)
    if scale is None:
        return eng.tensor_copy(out, in_)
    return eng.tensor_scalar(out, in_, scale, None, ALU.mult)


def matmuls(pe, out, pairs):
    for j, (lhsT, rhs) in enumerate(pairs):
        last = pe.matmul(out, lhsT, rhs, start=(j == 0), stop=(j == len(pairs) - 1))
    return last


def column_groups(M, tile, c0, width, xT, out, on="v", scale=None, rows=T, evac=None):
    w = M.weights.view(tile)
    k = w.shape[1]
    groups = []
    for r0 in range(0, rows, BANK):
        n = min(BANK, rows - r0)

        def pe(pe_, bank, r0=r0, n=n):
            return matmuls(pe_, bank[0:width, 0:n],
                           [(w[:, j, c0:c0 + width], xT[:, j, r0:r0 + n]) for j in range(k)])

        def ev(eng, bank, link, r0=r0, n=n):
            if evac:
                return evac(eng, bank[0:width, 0:n], link, r0, n)
            return move(eng, out[:, r0:r0 + n], bank[0:width, 0:n], scale)
        groups.append(group(pe, ev, on, tile))
    return groups


def row_groups(M, tile, c0, width, xT, outs, on="vs", rows=T, evac=None):
    w = M.weights.view(tile)
    k = w.shape[1]
    groups = []
    for t in range(rows // P):
        def pe(pe_, bank, t=t):
            return matmuls(pe_, bank[:, 0:width],
                           [(xT[:, j, t * P:(t + 1) * P], w[:, j, c0:c0 + width]) for j in range(k)])

        def ev(eng, bank, link, t=t):
            if evac:
                return evac(eng, bank[:, 0:width], link, t)
            return move(eng, outs(t), bank[:, 0:width])
        groups.append(group(pe, ev, on[t % len(on)], tile))
    return groups


def transposes(M, src, dst, rows, cols, on="vs", evac=None):
    groups = []
    for j in range(cols):
        for t0 in range(0, rows, 4):
            n = min(4, rows - t0)

            def pe(pe_, bank, j=j, t0=t0, n=n):
                for t in range(n):
                    last = pe_.transpose(bank[:, t * P:(t + 1) * P], src(t0 + t, j), M.ident[:, :])
                return last

            def ev(eng, bank, link, j=j, t0=t0, n=n):
                if evac:
                    return evac(eng, bank[:, 0:n * P], link, j, t0, n)
                return move(eng, dst(j, t0, n), bank[:, 0:n * P])
            groups.append(group(pe, ev, on[len(groups) % len(on)]))
    return groups


def attention(M, st, units, s_banks, nk_max, masked):
    nc, sig = M.nc, Signals(M.nc, st.name + "_att")
    N = len(units)
    scores = st.sb("scores", [P, 2, nk_max])
    probs_T = st.sb("probs_T", [P, 2, nk_max])
    stats = st.sb("stats", [P, 2, 8])
    o_banks = [7] if s_banks == 3 else [6, 7]
    t_banks = list(range(2 * s_banks, o_banks[0]))
    turns, done = [], 0
    for u in units:
        n = len(u.pv)
        turns.append([(done + j, 4 * j, min(4, n - 4 * j)) for j in range((n + 3) // 4)])
        done += len(turns[-1])
    turned_by = [t[-1][0] + 1 for t in turns]

    def s_view(i):
        b = (i % 2) * s_banks
        return M.ps[:, b:b + s_banks, :].rearrange("p b n -> p (b n)")

    with nc.Block() as block:
        @block.tensor
        def _(pe):
            def score(i):
                if i >= 2:
                    pe.wait_ge(sig["scores_taken"], i - 1)
                s, c = s_view(i), 0
                for j, (q, k, n, _) in enumerate(units[i].segs):
                    c0 = j * BANK if masked else c
                    last = pe.matmul(s[:, c0:c0 + n], q, k, start=True, stop=True)
                    c += n
                last.then_inc(sig["scored"], 1)

            def turn(i):
                pe.wait_ge(sig["exps"], i + 1)
                for g, c, n in turns[i]:
                    if g >= len(t_banks):
                        pe.wait_ge(sig["moved"], g - len(t_banks) + 1)
                    for x in range(n):
                        last = pe.transpose(M.ps[:, t_banks[g % len(t_banks)], x * P:(x + 1) * P],
                                            scores[:, i % 2, (c + x) * P:(c + x + 1) * P], M.ident[:, :])
                    last.then_inc(sig["turned"], 1)

            def weigh(i):
                pe.wait_ge(sig["moved"], turned_by[i])
                if i >= len(o_banks):
                    pe.wait_ge(sig["normed"], i - len(o_banks) + 1)
                matmuls(pe, M.ps[:, o_banks[i % len(o_banks)], 0:HD],
                        [(probs_T[:, i % 2, j * P:(j + 1) * P], v) for j, v in enumerate(units[i].pv)]
                        ).then_inc(sig["weighed"], 1)

            for i in range(N + 2):
                if i < N:
                    score(i)
                if i >= 2:
                    weigh(i - 2)
                if 1 <= i <= N:
                    turn(i - 1)

        @block.vector
        def _(dve):
            link = Chain(dve, sig["chain_v"])

            def maximum(i):
                dve.wait_ge(sig["scored"], i + 1)
                if i >= 2:
                    dve.wait_ge(sig["turned"], turned_by[i - 2])
                s, sl, c = s_view(i), i % 2, 0
                segs = units[i].segs
                if masked:
                    for j, (_, _, n, mask) in enumerate(segs):
                        last = dve.tensor_tensor_reduce(
                            scores[:, sl, c:c + n], s[:, j * BANK:j * BANK + n], mask, 1.0, -3.0e38,
                            ALU.add, ALU.max, stats[:, sl, j:j + 1])
                        c += n
                    last.then_inc(sig["scores_taken"], 1)
                    dve.wait_ge(sig["scores_taken"], i + 1)
                    dve.tensor_reduce(stats[:, sl, 3:4], stats[:, sl, 0:len(segs)], AX, ALU.max,
                                      negate=True).then_inc(sig["maxed"], 1)
                else:
                    n = sum(x[2] for x in segs)
                    dve.tensor_reduce(stats[:, sl, 3:4], s[:, 0:n], AX, ALU.max,
                                      negate=True).then_inc(sig["maxed"], 1)

            def norm(i):
                dve.wait_ge(sig["exps"], i + 1)
                link(dve.reciprocal(stats[:, i % 2, 5:6], stats[:, i % 2, 4:5]))
                dve.wait_ge(sig["weighed"], i + 1)
                dve.tensor_scalar(units[i].out, M.ps[:, o_banks[i % len(o_banks)], 0:HD],
                                  stats[:, i % 2, 5:6], None, ALU.mult).then_inc(sig["normed"], 1)

            for i in range(N + 2):
                if i >= 2:
                    norm(i - 2)
                if i < N:
                    maximum(i)

        @block.scalar
        def _(act):
            def exps(i):
                act.wait_ge(sig["maxed"], i + 1)
                sl, n = i % 2, sum(x[2] for x in units[i].segs)
                if i >= 2:
                    act.wait_ge(sig["turned"], turned_by[i - 2])
                src = scores[:, sl, 0:n] if masked else s_view(i)[:, 0:n]
                if i >= 2:
                    act.wait_ge(sig["normed"], i - 1)
                ins = act.activation(scores[:, sl, 0:n], src, ACT.Exp, bias=stats[:, sl, 3:4],
                                     accum_out=stats[:, sl, 4:5])
                ins.then_inc(sig["exps"], 1)

            def take(i):
                if not masked:
                    act.wait_ge(sig["exps"], i + 1)
                    act.sem_inc(sig["scores_taken"], 1)

            def out(i):
                if i >= 2:
                    act.wait_ge(sig["weighed"], i - 1)
                for g, c, n in turns[i]:
                    act.wait_ge(sig["turned"], g + 1)
                    act.activation(probs_T[:, i % 2, c * P:(c + n) * P],
                                   M.ps[:, t_banks[g % len(t_banks)], 0:n * P], ACT.Copy
                                   ).then_inc(sig["moved"], 1)

            for i in range(N + 1):
                if i < N:
                    exps(i)
                    take(i)
                if i >= 1:
                    out(i - 1)
    sig.close()


def layer_constants(M, st):
    nc, sig = M.nc, st.sig
    with nc.Block() as block:
        @block.gpsimd
        def _(pool):
            link = Chain(pool, sig["made"])

            def fill(ap, value):
                link(pool.memset(ap, value))

            def keep(ap, pattern, base, cm, fill_value, op=ALU.is_ge):
                link(pool.affine_select(out=ap, in_=ap, compare_op=op, fill=fill_value, base=base,
                                        pattern=pattern, channel_multiplier=cm))

            fill(M.ident[:, :], 0.0)
            keep(M.ident[:, :], [[-1, P]], 0, 1, 1.0, ALU.not_equal)
            fill(M.ones[:, :], 1.0)
            fill(M.causal[:, :], 0.0)
            keep(M.causal[:, :], [[-1, P]], 0, 1, NEG)


def load_x(M, st):
    nc, sig = M.nc, st.sig
    x_rows = st.sb("x_rows", [P, TT, D])

    def sync(sp):
        sp.dma_start(x_rows[:, :, :], M.A["x"].rearrange("o (t p) d -> p (o t) d", p=P)
                     ).then_inc(sig["x_in"], 16)
    gs = transposes(M, lambda t, j: x_rows[:, t, j * P:(j + 1) * P],
                    lambda j, t0, n: M.xT[:, j, t0 * P:(t0 + n) * P], TT, DK)
    first = gs[0].pe

    def first_pe(pe, bank):
        pe.wait_ge(sig["x_in"], 16)
        return first(pe, bank)
    gs[0].pe = first_pe
    products(M, "xT", gs, extra={"sync": sync})


def branch_a(M, oT):
    nc = M.nc
    dils = (1, 4, 16)
    with Stage(nc, "a") as st:
        qT = st.sb("qT", [P, 6, T])
        kT = st.sb("kT", [P, 6, T])
        v = st.sb("v", [P, TT, A_G * A_W])
        o = st.sb("o", [P, TT, A_W])
        seg = (2 * P, T, T)
        mask = [st.sb(f"mask{g}", [P, seg[g]]) for g in range(A_G)]
        residue = st.sb("residue", [P, 2, 16])
        t0 = M.weights.taken

        def masks(pool):
            link = Chain(pool, st.sig["masks"])
            for g, dil in enumerate(dils):
                n = seg[g]
                m = mask[g]
                if dil == 1:
                    link(pool.memset(m[:, :], 0.0))
                else:
                    link(pool.memset(residue[:, g - 1, :], NEG))
                    r = residue[:, g - 1, 0:dil]
                    for s in range(P // dil):
                        link(pool.affine_select(out=r, in_=r, compare_op=ALU.not_equal, fill=0.0,
                                                base=-dil * s, pattern=[[-1, dil]],
                                                channel_multiplier=1))
                    link(pool.tensor_copy(m[:, :].rearrange("p (a r) -> p a r", r=dil),
                                          r.unsqueeze(1).to_broadcast([P, n // dil, dil])))
                link(pool.affine_select(out=m[:, :], in_=m[:, :], compare_op=ALU.is_ge, fill=NEG,
                                        base=n - P, pattern=[[-1, n]], channel_multiplier=1))
            link(pool.affine_select(out=mask[0][:, :], in_=mask[0][:, :], compare_op=ALU.is_ge,
                                    fill=NEG, base=0, pattern=[[1, seg[0]]], channel_multiplier=-1))

        gs = []
        nq = A_G * A_W
        for c in range(0, 3 * nq, BANK):
            tile = t0 + c // BANK
            width = min(BANK, 3 * nq - c)
            while width > 0:
                lo = c
                if lo < 2 * nq:
                    dst = (qT if lo < nq else kT)[:, (lo % nq) // P, :]
                    gs += column_groups(M, tile, lo % BANK, P, M.xT, dst, "vs"[(lo // P) % 2],
                                        HD ** -0.5 if lo < nq else None)
                    step = P
                else:
                    step = width
                    gs += row_groups(M, tile, lo % BANK, step, M.xT,
                                     lambda t, lo=lo, n=step: v[:, t, lo - 2 * nq:lo - 2 * nq + n])
                c += step
                width -= step
        def zero_slots(pool):
            masks(pool)
            z = o[:, :, :].rearrange("p t n -> p (t n)")
            pool.memset(z, 0.0).then_inc(st.sig["zero"], 1)
            pool.wait_ge(st.sig["zero"], 1)
            for b in range(NBLK * EB // P):
                pool.dma_start(M.y_slot[b * P:(b + 1) * P, :], z).then_inc(st.sig["zeroed"], 16)
            pool.wait_ge(st.sig["zeroed"], NBLK * EB // P * 16)
        products(M, "a_in", gs, tiles=(3 * nq + BANK - 1) // BANK, extra={"gpsimd": zero_slots})
        units = []
        for h in range(A_H):
            hp, hc = (h % 2) * HD, h // 2
            for t in range(TT):
                segs, pv = [], []
                for g in range(A_G):
                    k0 = max(0, t - 1) if g == 0 else 0
                    n = (t + 1 - k0) * P
                    segs.append((qT[hp:hp + HD, 2 * g + hc, t * P:(t + 1) * P],
                                 kT[hp:hp + HD, 2 * g + hc, k0 * P:(t + 1) * P], n,
                                 mask[g][:, seg[g] - n:seg[g]]))
                    pv += [v[:, s, (g * A_H + h) * HD:(g * A_H + h + 1) * HD] for s in range(k0, t + 1)]
                units.append(Unit(segs=segs, pv=pv, out=o[:, t, h * HD:(h + 1) * HD]))
        attention(M, st, units, 3, seg[0] + 2 * T, True)
        gs = transposes(M, lambda t, j: o[:, t, j * P:(j + 1) * P],
                        lambda j, a, n: oT[:, j, a * P:(a + n) * P], TT, 2)
        products(M, "a_oT", gs)


def branch_b(M, oT):
    nc = M.nc
    with Stage(nc, "b") as st:
        qT = st.sb("qT", [P, 2, T])
        kT = st.sb("kT", [P, 2, T])
        v = st.sb("v", [P, TT, B_W])
        o = st.sb("o", [P, TT, B_W])
        iqT = st.sb("iqT", [P, 2, T])
        ikT = st.sb("ikT", [P, T])
        iw = st.sb("iw", [P, TT, 4])
        mask = st.sb("mask", [P, TT, T])
        t0 = M.weights.taken
        gs = []
        for c in range(4):
            gs += column_groups(M, t0, c * P, P, M.xT, (qT if c < 2 else kT)[:, c % 2, :], "vs"[c % 2],
                                HD ** -0.5 if c < 2 else None)
        gs += row_groups(M, t0 + 1, 0, B_W, M.xT, lambda t: v[:, t, :])
        for c in range(2):
            gs += column_groups(M, t0 + 1, B_W + c * P, P, M.xT, iqT[:, c, :], "vs"[c])
        w = M.weights.view(t0 + 2)
        for half in (0, HD):
            gs.append(group(
                lambda pe, bank, half=half: matmuls(
                    pe, bank[half:half + HD, :], [(w[:, j, 0:HD], M.xT[:, j, :]) for j in range(DK)]),
                lambda eng, bank, link, half=half: move(eng, ikT[half:half + HD, :], bank[half:half + HD, :]),
                "v" if half else "s", t0 + 2))
        gs += row_groups(M, t0 + 2, HD, 4, M.xT, lambda t: iw[:, t, :])
        products(M, "b_in", gs, tiles=3)
        index_masks(M, st, iqT, ikT, iw, mask)
        units = []
        for h in range(4):
            hp, hc = (h % 2) * HD, h // 2
            for t in range(TT):
                n = (t + 1) * P
                units.append(Unit(
                    segs=[(qT[hp:hp + HD, hc, t * P:n], kT[hp:hp + HD, hc, 0:n], n, mask[:, t, 0:n])],
                    pv=[v[:, s, h * HD:(h + 1) * HD] for s in range(t + 1)],
                    out=o[:, t, h * HD:(h + 1) * HD]))
        attention(M, st, units, 2, T, True)
        products(M, "b_oT", transposes(M, lambda t, j: o[:, t, j * P:(j + 1) * P],
                                       lambda j, a, n: oT[:, j, a * P:(a + n) * P], TT, 2))


def index_masks(M, st, iqT, ikT, iw, mask):
    nc, sig = M.nc, Signals(M.nc, "index")
    relu = st.sb("relu", [P, 4, T])
    top = st.sb("top", [P, 8])
    with nc.Block() as block:
        @block.tensor
        def _(pe):
            for t in range(1, TT):
                n = (t + 1) * P
                for h in range(4):
                    if t >= 3:
                        pe.wait_ge(sig["relus"], 4 * (t - 3) + h + 1)
                    pe.matmul(M.ps[:, 4 * (t % 2) + h, 0:n],
                              iqT[(h % 2) * HD:(h % 2 + 1) * HD, h // 2, t * P:n],
                              ikT[(h % 2) * HD:(h % 2 + 1) * HD, 0:n], start=True, stop=True
                              ).then_inc(sig["logits"], 1)

        @block.scalar
        def _(act):
            for t in range(1, TT):
                n = (t + 1) * P
                for h in range(4):
                    if t >= 2:
                        act.wait_ge(sig["weighted"], 4 * (t - 2) + h + 1)
                    act.wait_ge(sig["logits"], 4 * (t - 1) + h + 1)
                    act.activation(relu[:, h, 0:n], M.ps[:, 4 * (t % 2) + h, 0:n], ACT.Relu, scale=HD ** -0.5
                                   ).then_inc(sig["relus"], 1)

        @block.vector
        def _(dve):
            link = Chain(dve, sig["chain"])
            link(dve.tensor_copy(mask[:, 0, 0:P], M.causal[:, :]))
            for t in range(1, TT):
                n = (t + 1) * P
                s, diag = mask[:, t, 0:n], mask[:, t, n - P:n]
                for h in range(4):
                    dve.wait_ge(sig["relus"], 4 * (t - 1) + h + 1)
                    if h == 0:
                        dve.tensor_scalar(s, relu[:, h, 0:n], iw[:, t, h:h + 1], None, ALU.mult
                                          ).then_inc(sig["weighted"], 1)
                    else:
                        dve.wait_ge(sig["weighted"], 4 * (t - 1) + h)
                        dve.scalar_tensor_tensor(s, relu[:, h, 0:n], iw[:, t, h:h + 1], s, ALU.mult, ALU.add
                                                 ).then_inc(sig["weighted"], 1)
                dve.wait_ge(sig["weighted"], 4 * t)
                link(dve.tensor_tensor(diag, diag, M.causal[:, :], ALU.add))
                for _ in range(TOPK // 8):
                    link(dve.max(top[:, :], s))
                    link(dve.match_replace(s, top[:, :], s, -3.0e38))
                link(dve.tensor_scalar(s, s, -2.0e38, NEG, ALU.is_ge, ALU.mult))
                link(dve.tensor_tensor(diag, diag, M.causal[:, :], ALU.add))
    sig.close()


CH = 64
NCH = T // CH


def row_bcast(dram, n):
    return bass.AP(dram.tensor, dram.offset, [[0, P], [1, n]])


def rwkv_masks(M, st, upper, upper_eq, level, reset, heads, pair):
    def masks(pool):
        link = Chain(pool, st.sig["masks"])

        def keep(ap, pattern, base, cm, op=ALU.is_ge):
            link(pool.affine_select(out=ap, in_=ap, compare_op=op, fill=0.0, base=base,
                                    pattern=pattern, channel_multiplier=cm))

        for m, op in ((upper, ALU.is_gt), (upper_eq, ALU.is_ge), (heads, None)):
            link(pool.memset(m[:, :], 1.0))
            keep(m[:, :], [[-CH, 2], [0, CH]], 0, 1)
            keep(m[:, :], [[CH, 2], [0, CH]], CH - 1, -1)
            if op:
                keep(m[:, :], [[1, P]], 0, -1, op)
        for i in range(6):
            b = 1 << i
            m = level[:, i, :]
            link(pool.memset(m, 1.0))
            keep(m, [[-2 * b, P // (2 * b)], [0, 2 * b]], 0, 1)
            keep(m, [[2 * b, P // (2 * b)], [0, 2 * b]], b - 1, -1)
            keep(m, [[0, P // (2 * b)], [1, 2 * b]], -b, 0)
        link(pool.memset(reset[:, :], 1.0))
        link(pool.memset(reset[:, :].rearrange("p (c n) -> p c n", n=CH)[:, :, 0:1], 0.0))
        link(pool.memset(pair[:, :], 0.0))
        link(pool.memset(pair[0:HD, 0:1], 1.0))
        link(pool.memset(pair[HD:P, 1:2], 1.0))
    return masks


def branch_c(M, oT):
    nc, A = M.nc, M.A
    with Stage(nc, "c") as st:
        r_hat = st.sb("r_hat", [P, 2, T])
        a_hat = st.sb("a_hat", [P, 2, T])
        decay = st.sb("decay", [P, 2, T])
        b_rows = st.sb("b_rows", [P, TT, C_W])
        k_rows = st.sb("k_rows", [P, TT, C_W])
        v_rows = st.sb("v_rows", [P, TT, C_W])
        g_rows = st.sb("g_rows", [P, TT, C_W])
        bonus = st.sb("bonus", [P, TT, 4])
        level = st.sb("level", [P, 6, P])
        MT, NT, RBT, RKT = [st.sb(n, [P, 2, TT, 2, P]) for n in ("MT", "NT", "RBT", "RKT")]
        with Stage(nc, "c_pre") as sp_:
            upper = sp_.sb("upper", [P, P])
            upper_eq = sp_.sb("upper_eq", [P, P])
            heads = sp_.sb("heads", [P, P])
            pair = sp_.sb("pair", [P, 2])
            reset = sp_.sb("reset", [P, T])
            b_hat = sp_.sb("b_hat", [P, 2, T])
            k_hat = sp_.sb("k_hat", [P, 2, T])
            rk = sp_.sb("rk", [P, 2, T])
            mix = sp_.sb("mix", [P, 7, T])
            cols = sp_.sb("cols", [P, 5, 2])
            mu = sp_.sb("mu", [P, 7])
            lora = sp_.sb("lora", [P, C_W])
            with Stage(nc, "c_mix") as sm:
                pc = sm.sb("pc", [P, 7, T + 1])
                masks = rwkv_masks(M, sm, upper, upper_eq, level, reset, heads, pair)
                t0 = M.weights.taken

                def small(sp):
                    s = sm.sig["small"]
                    for j, n in enumerate(("c_w0", "c_a0", "c_kk", "c_ka", "c_rk")):
                        sp.dma_start(cols[:, j, :], A[n]).then_inc(s, 16)
                    sp.dma_start(mu[:, :], A["c_mu"]).then_inc(s, 16)
                    sp.dma_start(lora[0:32, :], A["c_w2"][0]).then_inc(s, 16)
                    sp.dma_start(lora[32:64, :], A["c_a2"][0]).then_inc(s, 16)
                    sp.dma_start(lora[64:P, :], A["c_g2"][0]).then_inc(s, 16)
                    sp.wait_ge(s, 9 * 16)

                gs = []
                for c in range(7):
                    gs += column_groups(M, t0 + c // 4, (c % 4) * P, P, M.xT, pc[:, c, 1:T + 1], "vs"[c % 2])
                products(M, "c_in", gs, tiles=2, extra={"sync": small, "gpsimd": masks})
                sig = Signals(nc, "c_shift")
                with nc.Block() as block:
                    @block.vector
                    def _(dve):
                        link = Chain(dve, sig["chain"])
                        link(dve.memset(pc[:, :, 0:1], 0.0))
                        for c in range(7):
                            link(dve.tensor_tensor(mix[:, c, :], pc[:, c, 0:T], pc[:, c, 1:T + 1], ALU.subtract))
                            link(dve.scalar_tensor_tensor(mix[:, c, :], mix[:, c, :], mu[:, c:c + 1],
                                                          pc[:, c, 1:T + 1], ALU.mult, ALU.add))
                sig.close()
            r, k, v, low = mix[:, 0:2, :], mix[:, 2:4, :], mix[:, 4:6, :], mix[:, 6, :]
            steps = [x for big in (MT, NT, RBT, RKT)
                     for x in (big[:, a, :, :, :].rearrange("p t h n -> p (t h n)")
                               .rearrange("p (c n) -> p c n", c=2) for a in range(2))]
            rwkv_operands(M, steps, r, k, low, cols, lora, heads, pair, reset,
                          r_hat, a_hat, b_hat, k_hat, rk, decay, g_rows, bonus)
            gs = []
            for src, dst in ((b_hat, b_rows), (k_hat, k_rows), (v, v_rows)):
                gs += transposes(M, lambda c, t, src=src: src[:, c, t * P:(t + 1) * P],
                                 lambda t, c0, n, dst=dst: dst[:, t, :], 2, TT, on="s")
            for dst, left, right, mask in ((MT, b_hat, a_hat, upper), (NT, k_hat, a_hat, upper),
                                           (RBT, b_hat, r_hat, upper_eq), (RKT, k_hat, r_hat, upper_eq)):
                for par in range(2):
                    for t2 in range(0, TT, 2):
                        def pe_(pe, bank, left=left, right=right, par=par, t2=t2):
                            for x in range(4):
                                t, hh = t2 + x // 2, x % 2
                                h0, s = par * HD, slice(t * P, (t + 1) * P)
                                last = pe.matmul(bank[:, x * P:(x + 1) * P], left[h0:h0 + HD, hh, s],
                                                 right[h0:h0 + HD, hh, s], start=True, stop=True)
                            return last

                        def ev(eng, bank, link, dst=dst, par=par, t2=t2, mask=mask):
                            return eng.tensor_tensor(
                                dst[:, par, t2:t2 + 2, :, :].rearrange("p t h n -> p (t h) n"),
                                bank.rearrange("p (x n) -> p x n", n=P),
                                mask[:, :].unsqueeze(1).to_broadcast([P, 4, P]), ALU.mult)
                        gs.append(group(pe_, ev, "v"))
            products(M, "c_tok", gs)
        with Stage(nc, "c_inv") as si:
            inv_T = si.sb("inv_T", [P, 16, P])
            with Stage(nc, "c_dbl") as sd:
                rwkv_inverse(M, sd, MT, level, inv_T)
            y = si.sb("y", [P, TT, C_W])
            with Stage(nc, "c_seq") as ss:
                rwkv_scan(M, ss, r_hat, a_hat, decay, b_rows, k_rows, v_rows, NT, RBT, RKT, inv_T, y)
            with Stage(nc, "c_out") as so:
                rwkv_output(M, so, y, v_rows, g_rows, bonus)
            products(M, "c_oT", transposes(M, lambda t, j: y[:, t, j * P:(j + 1) * P],
                                           lambda j, a, n: oT[:, j, a * P:(a + n) * P], TT, 2))


def rwkv_operands(M, steps, r, k, low, cols, lora, heads, pair, reset,
                  r_hat, a_hat, b_hat, k_hat, rk, decay, g_rows, bonus):
    nc, sig = M.nc, Signals(M.nc, "c_oper")
    act_low = steps[0][:, 0, :]
    ld = steps[1]
    cs = steps[2]
    a, kk, tmp = steps[3], steps[4], steps[5]
    grow = steps[6]
    prev = steps[7]
    with nc.Block() as block:
        @block.scalar
        def _(act):
            act.activation(act_low[0:32, :], low[0:32, :], ACT.Tanh).then_inc(sig["lows"], 1)
            act.activation(act_low[64:P, :], low[64:P, :], ACT.Sigmoid).then_inc(sig["lows"], 1)
            act.wait_ge(sig["rates"], 4)
            for c in range(2):
                act.activation(ld[:, c, :], M.ps[:, c, :], ACT.Sigmoid, bias=cols[:, 0, c:c + 1]
                               ).then_inc(sig["sigmoids"], 1)
                act.activation(a[:, c, :], M.ps[:, 2 + c, :], ACT.Sigmoid, bias=cols[:, 1, c:c + 1]
                               ).then_inc(sig["sigmoids"], 1)
            act.wait_ge(sig["gates"], 4)
            for t in range(TT):
                act.activation(g_rows[:, t, :], M.ps[:, 4 + t, 0:C_W], ACT.Copy).then_inc(sig["gates_out"], 1)
            act.wait_ge(sig["norms"], 2)
            for c in range(2):
                act.activation(tmp[:, c, :], M.ps[:, c, :], ACT.Sqrt).then_inc(sig["lengths"], 1)
            act.wait_ge(sig["sums"], 2)
            act.activation(decay[:, :, :], cs[:, :, :], ACT.Exp).then_inc(sig["decays"], 1)
            act.activation(grow[:, :, :], cs[:, :, :], ACT.Exp, scale=-1.0).then_inc(sig["decays"], 1)
            act.activation(prev[:, :, :], prev[:, :, :], ACT.Exp).then_inc(sig["decays"], 1)

        @block.tensor
        def _(pe):
            pe.wait_ge(sig["lows"], 2)
            for c in range(2):
                pe.matmul(M.ps[:, c, :], lora[0:32, c * P:(c + 1) * P], act_low[0:32, :],
                          start=True, stop=True).then_inc(sig["rates"], 1)
                pe.matmul(M.ps[:, 2 + c, :], lora[32:64, c * P:(c + 1) * P], low[32:64, :],
                          start=True, stop=True).then_inc(sig["rates"], 1)
            for t in range(TT):
                pe.matmul(M.ps[:, 4 + t, 0:C_W], act_low[64:P, t * P:(t + 1) * P], lora[64:P, :],
                          start=True, stop=True).then_inc(sig["gates"], 1)
            pe.wait_ge(sig["squares"], 1)
            pe.wait_ge(sig["sigmoids"], 4)
            for c in range(2):
                pe.matmul(M.ps[:, c, :], heads[:, :], tmp[:, c, :], start=True, stop=True
                          ).then_inc(sig["norms"], 1)
            pe.wait_ge(sig["bonus_in"], 1)
            pe.wait_ge(sig["gates_out"], 4)
            for t in range(TT):
                for c in range(2):
                    last = pe.matmul(M.ps[:, 4, 4 * t + 2 * c:4 * t + 2 * c + 2], rk[:, c, t * P:(t + 1) * P],
                                     pair[:, :], start=True, stop=True)
            last.then_inc(sig["bonus_sum"], 1)

        @block.vector
        def _(dve):
            link = Chain(dve, sig["chain"])
            for c in range(2):
                link(dve.tensor_scalar(kk[:, c, :], k[:, c, :], cols[:, 2, c:c + 1], None, ALU.mult))
            dve.tensor_tensor(tmp[:, :, :], kk[:, :, :], kk[:, :, :], ALU.mult).then_inc(sig["squares"], 1)
            dve.wait_ge(sig["sigmoids"], 4)
            link(dve.tensor_scalar(ld[:, :, :], ld[:, :, :], -0.6065306597126334, None, ALU.mult))
            for c in range(2):
                dve.tensor_tensor_scan(cs[:, c, :], reset[:, :], ld[:, c, :], 0.0, ALU.mult, ALU.add
                                       ).then_inc(sig["scans"], 1)
            dve.wait_ge(sig["scans"], 2)
            for c in range(2):
                dve.tensor_tensor(prev[:, c, :], cs[:, c, :], ld[:, c, :], ALU.subtract
                                  ).then_inc(sig["sums"], 1)
            for c in range(2):
                link(dve.tensor_scalar(k_hat[:, c, :], a[:, c, :], 1.0, cols[:, 3, c:c + 1],
                                       ALU.subtract, ALU.mult))
                link(dve.scalar_tensor_tensor(k_hat[:, c, :], k_hat[:, c, :], 1.0, k[:, c, :],
                                              ALU.add, ALU.mult))
                link(dve.scalar_tensor_tensor(rk[:, c, :], r[:, c, :], cols[:, 4, c:c + 1], k_hat[:, c, :],
                                              ALU.mult, ALU.mult))
            dve.sem_inc(sig["bonus_in"], 1)
            dve.wait_ge(sig["lengths"], 2)
            link(dve.tensor_scalar(tmp[:, :, :], tmp[:, :, :], 1e-12, None, ALU.max))
            link(dve.reciprocal(tmp[:, :, :], tmp[:, :, :]))
            link(dve.tensor_tensor(kk[:, :, :], kk[:, :, :], tmp[:, :, :], ALU.mult))
            dve.wait_ge(sig["decays"], 3)
            link(dve.tensor_tensor(k_hat[:, :, :], k_hat[:, :, :], grow[:, :, :], ALU.mult))
            link(dve.tensor_tensor(r_hat[:, :, :], r, decay[:, :, :], ALU.mult))
            for c in range(2):
                link(dve.scalar_tensor_tensor(a_hat[:, c, :], kk[:, c, :], -1.0, prev[:, c, :],
                                              ALU.mult, ALU.mult))
            link(dve.tensor_tensor(a[:, :, :], a[:, :, :], kk[:, :, :], ALU.mult))
            link(dve.tensor_tensor(b_hat[:, :, :], a[:, :, :], grow[:, :, :], ALU.mult))
            dve.wait_ge(sig["bonus_sum"], 1)
            link(dve.tensor_copy(bonus[:, :, :], M.ps[:, 4, 0:16].rearrange("p (t h) -> p t h", h=4)))
    sig.close()


def rwkv_inverse(M, st, MT, level, inv_T):
    nc, sig = M.nc, Signals(M.nc, "c_double")
    m = MT[:, :, :, :, :].rearrange("p a t h n -> p (a t h) n")
    inv = st.sb("inv", [P, 16, P])
    xT = st.sb("xT", [P, 16, P])
    xz = st.sb("xz", [P, 16, P])

    def four(buf, q):
        return buf[:, 4 * q:4 * q + 4, :]

    def bank(b):
        return M.ps[:, b, :].rearrange("p (x n) -> p x n", n=P)

    with nc.Block() as block:
        @block.tensor
        def _(pe):
            for lv in range(6):
                for q in range(4):
                    pe.wait_ge(sig["quarters"], 4 * lv + q + 1)
                    pe.wait_ge(sig["inv"], 4 * lv + q + 1)
                    pe.wait_ge(sig["inv_T"], 4 * lv + q + 1)
                    for x in range(4):
                        last = pe.matmul(bank(q)[:, x, :], xT[:, 4 * q + x, :], inv[:, 4 * q + x, :],
                                         start=True, stop=True)
                    last.then_inc(sig["xz_made"], 1)
                for q in range(4):
                    pe.wait_ge(sig["xz"], 4 * lv + q + 1)
                    for x in range(4):
                        last = pe.matmul(bank(4 + q)[:, x, :], inv_T[:, 4 * q + x, :], xz[:, 4 * q + x, :],
                                         start=True, stop=True)
                    last.then_inc(sig["zxz"], 1)
                for q in range(4):
                    for x in range(4):
                        last = pe.matmul(bank(q)[:, x, :], xz[:, 4 * q + x, :], inv_T[:, 4 * q + x, :],
                                         start=True, stop=True)
                    last.then_inc(sig["zxz_T"], 1)

        @block.scalar
        def _(act):
            for lv in range(6):
                for q in range(4):
                    if lv:
                        act.wait_ge(sig["zxz_T"], 4 * (lv - 1) + q + 1)
                    act.wait_ge(sig["xz_made"], 4 * lv + q + 1)
                    act.activation(four(xz, q), bank(q), ACT.Copy).then_inc(sig["xz"], 1)

        @block.vector
        def _(dve):
            def quarters(lv):
                for q in range(4):
                    if lv:
                        dve.wait_ge(sig["xz_made"], 4 * (lv - 1) + q + 1)
                    dve.tensor_tensor(four(xT, q), four(m, q),
                                      level[:, lv, :].unsqueeze(1).to_broadcast([P, 4, P]), ALU.mult
                                      ).then_inc(sig["quarters"], 1)

            eye = M.ident[:, :].unsqueeze(1).to_broadcast([P, 4, P])
            for q in range(4):
                dve.tensor_copy(four(inv, q), eye).then_inc(sig["inv"], 1)
                dve.tensor_copy(four(inv_T, q), eye).then_inc(sig["inv_T"], 1)
            quarters(0)
            for lv in range(6):
                for q in range(4):
                    dve.wait_ge(sig["zxz"], 4 * lv + q + 1)
                    dve.wait_ge(sig["inv"], 4 * lv + q + 1)
                    dve.tensor_tensor(four(inv, q), bank(4 + q), four(inv, q), ALU.add).then_inc(sig["inv"], 1)
                if lv < 5:
                    quarters(lv + 1)
                for q in range(4):
                    dve.wait_ge(sig["zxz_T"], 4 * lv + q + 1)
                    dve.wait_ge(sig["inv_T"], 4 * lv + q + 1)
                    dve.tensor_tensor(four(inv_T, q), bank(q), four(inv_T, q), ALU.add
                                      ).then_inc(sig["inv_T"], 1)
    sig.close()


def rwkv_scan(M, st, r_hat, a_hat, decay, b_rows, k_rows, v_rows, NT, RBT, RKT, inv_T, y):
    nc, sig = M.nc, Signals(M.nc, "c_scan")
    u0 = st.sb("u0", [P, TT, C_W])
    u = st.sb("u", [P, TT, C_W])
    state = st.sb("state", [P, 2, 4, HD])
    faded = st.sb("faded", [P, 4, HD])

    def token(buf, t, h, pb):
        return buf[:, h % 2, t, h // 2, pb:pb + CH]

    with nc.Block() as block:
        @block.tensor
        def _(pe):
            for c in range(NCH):
                t, pb = c // 2, (c % 2) * CH
                now = slice(c * CH, (c + 1) * CH)
                s, par = state[:, c % 2, :, :], c % 2
                pe.wait_ge(sig["state"], 4 * (c + 1))
                if c == 0:
                    pe.wait_ge(sig["zeros"], 2)
                b = M.ps[:, par, :]
                if c >= 2:
                    pe.wait_ge(sig["u0"], c - 1)
                for h in range(4):
                    out = b[pb:pb + CH, h * HD:(h + 1) * HD]
                    pe.matmul(out, a_hat[:, h // 2, now], s[:, h, :], start=True, stop=False)
                    last = pe.matmul(out, token(NT, t, h, pb), v_rows[:, t, h * HD:(h + 1) * HD],
                                     start=False, stop=True)
                last.then_inc(sig["u0_made"], 1)
                pe.wait_ge(sig["u0"], c + 1)
                if c >= 2:
                    pe.wait_ge(sig["u"], c - 1)
                for h in range(4):
                    last = pe.matmul(M.ps[pb:pb + CH, 2 + par, h * HD:(h + 1) * HD],
                                     inv_T[:, 8 * (h % 2) + 2 * t + h // 2, pb:pb + CH],
                                     u0[:, t, h * HD:(h + 1) * HD], start=True, stop=True)
                last.then_inc(sig["u_made"], 1)
                pe.wait_ge(sig["u"], c + 1)
                if c + 1 < NCH:
                    for h in range(4):
                        out = M.ps[:, 4 + par, h * HD:(h + 1) * HD]
                        two = slice((h // 2) * P, (h // 2 + 1) * P)
                        one = slice(h * HD, (h + 1) * HD)
                        pe.matmul(out, b_rows[pb:pb + CH, t, two], u[pb:pb + CH, t, one], start=True, stop=False)
                        last = pe.matmul(out, k_rows[pb:pb + CH, t, two], v_rows[pb:pb + CH, t, one],
                                         start=False, stop=True)
                    last.then_inc(sig["state_made"], 1)
                if c >= 2:
                    pe.wait_ge(sig["y"], c - 1)
                for h in range(4):
                    out = M.ps[pb:pb + CH, 6 + par, h * HD:(h + 1) * HD]
                    one = slice(h * HD, (h + 1) * HD)
                    pe.matmul(out, r_hat[:, h // 2, now], s[:, h, :], start=True, stop=False)
                    pe.matmul(out, token(RBT, t, h, pb), u[:, t, one], start=False, stop=False)
                    last = pe.matmul(out, token(RKT, t, h, pb), v_rows[:, t, one], start=False, stop=True)
                last.then_inc(sig["y_made"], 1)

        @block.scalar
        def _(act):
            for c in range(NCH):
                t, pb = c // 2, (c % 2) * CH
                act.wait_ge(sig["y_made"], c + 1)
                act.activation(y[pb:pb + CH, t, :], M.ps[pb:pb + CH, 6 + c % 2, 0:C_W], ACT.Copy
                               ).then_inc(sig["y"], 1)

        @block.vector
        def _(dve):
            dve.memset(u0[:, :, :], 0.0).then_inc(sig["zeros"], 1)
            dve.memset(u[:, :, :], 0.0).then_inc(sig["zeros"], 1)
            dve.memset(state[:, :, :, :], 0.0).then_inc(sig["state"], 4)
            dve.wait_ge(sig["zeros"], 2)
            for c in range(NCH):
                t, pb, par = c // 2, (c % 2) * CH, c % 2
                end = (c + 1) * CH - 1
                if c + 1 < NCH:
                    dve.wait_ge(sig["state"], 4 * (c + 1))
                    for h in range(4):
                        h0 = (h % 2) * HD
                        dve.tensor_scalar(faded[h0:h0 + HD, h, :], state[h0:h0 + HD, par, h, :],
                                          decay[h0:h0 + HD, h // 2, end:end + 1], None, ALU.mult
                                          ).then_inc(sig["faded"], 1)
                dve.wait_ge(sig["u0_made"], c + 1)
                dve.tensor_copy(u0[pb:pb + CH, t, :], M.ps[pb:pb + CH, par, 0:C_W]).then_inc(sig["u0"], 1)
                dve.wait_ge(sig["u_made"], c + 1)
                dve.tensor_copy(u[pb:pb + CH, t, :], M.ps[pb:pb + CH, 2 + par, 0:C_W]).then_inc(sig["u"], 1)
                if c + 1 < NCH:
                    dve.wait_ge(sig["state_made"], c + 1)
                    if c:
                        dve.wait_ge(sig["y_made"], c)
                    dve.wait_ge(sig["faded"], 4 * (c + 1))
                    for h in range(4):
                        h0 = (h % 2) * HD
                        dve.scalar_tensor_tensor(
                            state[h0:h0 + HD, 1 - par, h, :], M.ps[h0:h0 + HD, 4 + par, h * HD:(h + 1) * HD],
                            decay[h0:h0 + HD, h // 2, end:end + 1], faded[h0:h0 + HD, h, :],
                            ALU.mult, ALU.add).then_inc(sig["state"], 1)
    sig.close()


def rwkv_output(M, st, y, v_rows, g_rows, bonus):
    nc, A, sig = M.nc, M.A, Signals(M.nc, "c_norm")
    gw = st.sb("gw", [P, C_W])
    gb = st.sb("gb", [P, C_W])
    sq = st.sb("sq", [P, 16, HD])
    s = st.sb("s", [P, 3, 16])
    eps = st.sb("eps", [P, 1])
    yh = y[:, :, :].rearrange("p t (h n) -> p (t h) n", n=HD)
    vh = v_rows[:, :, :].rearrange("p t (h n) -> p (t h) n", n=HD)

    def per_head(x):
        return x.unsqueeze(2).to_broadcast([P, 16, HD])

    def per_tile(x):
        return x[:, :].unsqueeze(1).to_broadcast([P, TT, C_W])

    with nc.Block() as block:
        @block.sync
        def _(sp):
            sp.dma_start(gw[:, :], row_bcast(A["c_gn_w"][0], C_W)).then_inc(sig["gains"], 16)
            sp.dma_start(gb[:, :], row_bcast(A["c_gn_b"][0], C_W)).then_inc(sig["gains"], 16)

        @block.scalar
        def _(act):
            act.wait_ge(sig["var"], 1)
            act.activation(s[:, 1, :], s[:, 1, :], ACT.Sqrt, bias=eps[:, :], scale=1.0 / HD
                           ).then_inc(sig["std"], 1)

        @block.vector
        def _(dve):
            link = Chain(dve, sig["chain"])
            link(dve.memset(eps[:, :], 64e-5))
            link(dve.tensor_reduce(s[:, 0, :], yh, AX, ALU.add))
            link(dve.tensor_scalar(s[:, 0, :], s[:, 0, :], 1.0 / HD, None, ALU.mult))
            link(dve.tensor_tensor(yh, yh, per_head(s[:, 0, :]), ALU.subtract))
            link(dve.tensor_tensor(sq[:, :, :], yh, yh, ALU.mult))
            dve.tensor_reduce(s[:, 1, :], sq[:, :, :], AX, ALU.add).then_inc(sig["var"], 1)
            dve.wait_ge(sig["std"], 1)
            link(dve.reciprocal(s[:, 2, :], s[:, 1, :]))
            link(dve.tensor_tensor(yh, yh, per_head(s[:, 2, :]), ALU.mult))
            dve.wait_ge(sig["gains"], 32)
            link(dve.tensor_tensor(y[:, :, :], y[:, :, :], per_tile(gw), ALU.mult))
            link(dve.tensor_tensor(y[:, :, :], y[:, :, :], per_tile(gb), ALU.add))
            link(dve.tensor_tensor(sq[:, :, :], vh, per_head(bonus[:, :, :].rearrange("p t h -> p (t h)")),
                                   ALU.mult))
            link(dve.tensor_tensor(yh, yh, sq[:, :, :], ALU.add))
            link(dve.tensor_tensor(y[:, :, :], y[:, :, :], g_rows[:, :, :], ALU.mult))
    sig.close()


def branch_d(M, oT):
    nc, A = M.nc, M.A
    with Stage(nc, "ssm") as st:
        xbc = st.sb("xbc", [P, 4, T])
        silu_z = st.sb("silu_z", [P, TT, 256])
        x_rows = st.sb("x_rows", [P, TT, 256])
        xdt = st.sb("xdt", [P, TT, 256])
        y = st.sb("y", [P, TT, 256])
        dt_raw = st.sb("dt_raw", [4, T])
        small = st.sb("small", [4, 2])
        cw = st.sb("cw", [P, 4, 4])
        cb = st.sb("cb", [P, 4])
        skip = st.sb("skip", [P, 4])
        nw = st.sb("nw", [P, 256])
        mask = st.sb("mask", [P, P])
        dtl = st.sb("dtl", [4, 2, T])
        dtl_rows = st.sb("dtl_rows", [P, 2, TT, 4])
        L_all = st.sb("L_all", [P, 4, T])
        with Stage(nc, "d_conv") as sc:
            pre = sc.sb("pre", [P, 4, T + 3])
            t0 = M.weights.taken

            def loads(sp):
                s = sc.sig["loads"]
                sp.dma_start(small[:, 0:1], A["d_dt_bias"].rearrange("o h -> h o")).then_inc(s, 16)
                sp.dma_start(small[:, 1:2], A["d_a_log"].rearrange("o h -> h o")).then_inc(s, 16)
                sp.dma_start(cw[:, :, :], A["d_conv_w"]).then_inc(s, 16)
                sp.dma_start(cb[:, :], A["d_conv_b"]).then_inc(s, 16)
                sp.dma_start(skip[:, :], row_bcast(A["d_skip"][0], 4)).then_inc(s, 16)
                sp.dma_start(nw[:, :], row_bcast(A["d_norm_w"][0], 256)).then_inc(s, 16)
                sp.wait_ge(s, 6 * 16)

            def masks(pool):
                link = Chain(pool, sc.sig["masks"])
                link(pool.memset(mask[:, :], 1.0))
                link(pool.affine_select(out=mask[:, :], in_=mask[:, :], compare_op=ALU.is_ge, fill=0.0,
                                        base=0, pattern=[[1, P]], channel_multiplier=-1))
                link(pool.memset(pre[:, :, 0:3], 0.0))

            gs = row_groups(M, t0, 0, 256, M.xT, None, on="s", evac=lambda eng, bank, link, t:
                            eng.activation(silu_z[:, t, :], bank, ACT.Silu))
            for c in range(4):
                gs += column_groups(M, t0 + c // 2, (256 + c * P) % BANK, P, M.xT, pre[:, c, 3:T + 3], "v")
            gs += column_groups(M, t0 + 1, 256, 4, M.xT, dt_raw[:, :], "v")
            products(M, "d_in", gs, tiles=2, extra={"sync": loads, "gpsimd": masks})
            mamba_conv(M, pre, cw, cb, xbc, dt_raw, small, dtl)
        products(M, "d_rows",
                 transposes(M, lambda c, t: xbc[:, c, t * P:(t + 1) * P], lambda t, c0, n: x_rows[:, t, :],
                            2, TT)
                 + [group(lambda pe, bank: dtl_turned(pe, M, dtl, bank),
                          lambda eng, bank, link: eng.tensor_copy(
                              dtl_rows[:, :, :, :].rearrange("p a t h -> p (a t h)"), bank[:, 0:32]), "v")],
                 extra={"sync": lambda sp: spread_L(sp, M, st, dtl, L_all)})
        with Stage(nc, "d_ssd") as ss:
            mamba_ssd(M, ss, xbc, x_rows, dtl_rows, L_all, xdt, mask, skip, y)
        with Stage(nc, "d_out") as so:
            mamba_output(M, so, y, silu_z, nw)
        products(M, "d_oT", transposes(M, lambda t, j: y[:, t, j * P:(j + 1) * P],
                                       lambda j, a, n: oT[:, j, a * P:(a + n) * P], TT, 2))


def dtl_turned(pe, M, dtl, bank):
    for a in range(2):
        for t in range(TT):
            last = pe.transpose(bank[:, (a * TT + t) * 4:(a * TT + t) * 4 + 4], dtl[:, a, t * P:(t + 1) * P],
                                M.ident[0:4, 0:4])
    return last


def spread_L(sp, M, st, dtl, L_all):
    sp.dma_start(M.scratch_L, dtl[:, 1, :]).then_inc(st.sig["L_out"], 16)
    sp.wait_ge(st.sig["L_out"], 16)
    sp.dma_start(L_all[:, :, :].rearrange("p h t -> p (h t)"),
                 bass.AP(M.scratch_L.tensor, M.scratch_L.offset, [[0, P], [1, 4 * T]])
                 ).then_inc(st.sig["L_in"], 16)
    sp.wait_ge(st.sig["L_in"], 16)


def mamba_conv(M, pre, cw, cb, xbc, dt_raw, small, dtl):
    nc, sig = M.nc, Signals(M.nc, "d_conv1")
    with Stage(nc, "d_dt") as st:
        s = st.sb("s", [4, 5, T])
        x, e, u, d, ln = (s[:, i, :] for i in range(5))
        one = st.sb("one", [4, T])
        with nc.Block() as block:
            @block.vector
            def _(dve):
                link = Chain(dve, sig["chain"])
                dve.tensor_scalar(x, dt_raw[:, :], small[:, 0:1], None, ALU.add).then_inc(sig["x"], 1)
                for c in range(4):
                    link(dve.tensor_scalar(xbc[:, c, :], pre[:, c, 0:T], cw[:, c, 0:1], cb[:, c:c + 1],
                                           ALU.mult, ALU.add))
                    for w in range(1, 4):
                        link(dve.scalar_tensor_tensor(xbc[:, c, :], pre[:, c, w:w + T], cw[:, c, w:w + 1],
                                                      xbc[:, c, :], ALU.mult, ALU.add))
                dve.sem_inc(sig["conv"], 1)
                dve.wait_ge(sig["exp"], 2)
                link(dve.tensor_scalar(u, e, 1.0, None, ALU.add))
                dve.tensor_scalar(d, u, 1.0, None, ALU.subtract).then_inc(sig["u"], 1)
                dve.wait_ge(sig["u"], 1)
                dve.wait_ge(sig["ln"], 1)
                link(dve.tensor_scalar(u, d, 0.0, None, ALU.is_equal))
                link(dve.tensor_scalar(d, d, 1e-30, None, ALU.max))
                link(dve.reciprocal(d, d))
                link(dve.tensor_tensor(ln, ln, d, ALU.mult))
                link(dve.tensor_tensor(ln, ln, u, ALU.add))
                link(dve.tensor_tensor(ln, ln, e, ALU.mult))
                link(dve.scalar_tensor_tensor(dtl[:, 0, :], x, 0.0, ln, ALU.max, ALU.add))
                link(dve.tensor_scalar(small[:, 1:2], small[:, 1:2], -1.0, None, ALU.mult))
                link(dve.tensor_scalar(ln, dtl[:, 0, :], small[:, 1:2], None, ALU.mult))
                link(dve.memset(one[:, :], 1.0))
                link(dve.tensor_tensor_scan(dtl[:, 1, :], one[:, :], ln, 0.0, ALU.mult, ALU.add))

            @block.scalar
            def _(act):
                act.activation(small[:, 1:2], small[:, 1:2], ACT.Exp).then_inc(sig["exp"], 1)
                act.wait_ge(sig["x"], 1)
                act.activation(e, x, ACT.Abs).then_inc(sig["abs"], 1)
                act.wait_ge(sig["abs"], 1)
                act.activation(e, e, ACT.Exp, scale=-1.0).then_inc(sig["exp"], 1)
                act.wait_ge(sig["u"], 1)
                act.activation(ln, u, ACT.Ln).then_inc(sig["ln"], 1)
                act.wait_ge(sig["conv"], 1)
                act.activation(xbc[:, :, :], xbc[:, :, :], ACT.Silu).then_inc(sig["silu"], 1)
        sig.close()


def mamba_ssd(M, st, xbc, x_rows, dtl_rows, L_all, xdt, mask, skip, y):
    nc, sig = M.nc, Signals(M.nc, "d_ssd1")
    fade = st.sb("fade", [P, 2, T])
    wts = st.sb("wts", [P, 2, TT, T])
    units = [(h, s) for h in range(4) for s in range(TT)]
    with nc.Block() as block:
        @block.tensor
        def _(pe):
            def outputs(pe, h):
                pe.wait_ge(sig["weights"], TT * (h + 1))
                pe.wait_ge(sig["xdt"], 1)
                if h >= 2:
                    pe.wait_ge(sig["y"], h - 1)
                for t in range(TT):
                    last = matmuls(pe, M.ps[:, 4 + h % 2, t * HD:(t + 1) * HD],
                                   [(wts[:, h % 2, s, (t - s) * P:(t - s + 1) * P], xdt[:, s, h * HD:(h + 1) * HD])
                                    for s in range(t + 1)])
                last.then_inc(sig["y_made"], 1)

            for i, (h, s) in enumerate(units):
                g0, n = (h // 2) * HD, T - s * P
                if i >= 4:
                    pe.wait_ge(sig["weights"], i - 3)
                pe.matmul(M.ps[:, i % 4, 0:n], xbc[g0:g0 + HD, 2, s * P:(s + 1) * P],
                          xbc[g0:g0 + HD, 3, s * P:T], start=True, stop=True).then_inc(sig["scores"], 1)
                if s == TT - 1 and h >= 1:
                    outputs(pe, h - 1)
            outputs(pe, 3)

        @block.scalar
        def _(act):
            for i, (h, s) in enumerate(units):
                n = T - s * P
                act.wait_ge(sig["gaps"], i + 1)
                act.activation(fade[:, i % 2, 0:n], fade[:, i % 2, 0:n], ACT.Exp).then_inc(sig["faded"], 1)

        @block.vector
        def _(dve):
            link = Chain(dve, sig["chain"])
            dt = dtl_rows[:, 0, :, :].rearrange("p t h -> p (t h)")
            dve.tensor_tensor(xdt[:, :, :].rearrange("p t (h n) -> p (t h) n", n=HD),
                              x_rows[:, :, :].rearrange("p t (h n) -> p (t h) n", n=HD),
                              dt.unsqueeze(2).to_broadcast([P, 16, HD]), ALU.mult).then_inc(sig["xdt"], 1)

            def gaps(i):
                h, s = units[i]
                n = T - s * P
                if i >= 2:
                    dve.wait_ge(sig["weights"], i - 1)
                dve.tensor_scalar(fade[:, i % 2, 0:n], L_all[:, h, s * P:T], dtl_rows[:, 1, s, h:h + 1], 0.0,
                                  ALU.subtract, ALU.min).then_inc(sig["gaps"], 1)

            def skips(h):
                dve.wait_ge(sig["y_made"], h + 1)
                dve.scalar_tensor_tensor(y[:, :, h * HD:(h + 1) * HD], x_rows[:, :, h * HD:(h + 1) * HD],
                                         skip[:, h:h + 1],
                                         M.ps[:, 4 + h % 2, 0:TT * HD].rearrange("p (t n) -> p t n", n=HD),
                                         ALU.mult, ALU.add).then_inc(sig["y"], 1)

            gaps(0)
            for i, (h, s) in enumerate(units):
                n = T - s * P
                if i + 1 < len(units):
                    gaps(i + 1)
                dve.wait_ge(sig["scores"], i + 1)
                dve.wait_ge(sig["faded"], i + 1)
                if h >= 2:
                    dve.wait_ge(sig["y_made"], h - 1)
                link(dve.tensor_tensor(wts[:, h % 2, s, 0:n], fade[:, i % 2, 0:n], M.ps[:, i % 4, 0:n],
                                       ALU.mult))
                dve.tensor_tensor(wts[:, h % 2, s, 0:P], wts[:, h % 2, s, 0:P], mask[:, :], ALU.mult
                                  ).then_inc(sig["weights"], 1)
                if s == TT - 1 and h >= 1:
                    skips(h - 1)
            skips(3)
    sig.close()


def mamba_output(M, st, y, silu_z, nw):
    nc, sig = M.nc, Signals(M.nc, "d_norm")
    sq = st.sb("sq", [P, 8, P])
    s = st.sb("s", [P, 2, 8])
    eps = st.sb("eps", [P, 1])
    yg = y[:, :, :].rearrange("p t (g n) -> p (t g) n", n=P)
    with nc.Block() as block:
        @block.scalar
        def _(act):
            act.wait_ge(sig["var"], 1)
            act.activation(s[:, 0, :], s[:, 0, :], ACT.Sqrt, bias=eps[:, :], scale=1.0 / P
                           ).then_inc(sig["std"], 1)

        @block.vector
        def _(dve):
            link = Chain(dve, sig["chain"])
            link(dve.memset(eps[:, :], 1e-5))
            link(dve.tensor_tensor(y[:, :, :], y[:, :, :], silu_z[:, :, :], ALU.mult))
            link(dve.tensor_tensor(sq[:, :, :], yg, yg, ALU.mult))
            dve.tensor_reduce(s[:, 0, :], sq[:, :, :], AX, ALU.add).then_inc(sig["var"], 1)
            dve.wait_ge(sig["std"], 1)
            link(dve.reciprocal(s[:, 1, :], s[:, 0, :]))
            link(dve.tensor_tensor(yg, yg, s[:, 1, :].unsqueeze(2).to_broadcast([P, 8, P]), ALU.mult))
            link(dve.tensor_tensor(y[:, :, :], y[:, :, :], nw[:, :].unsqueeze(1).to_broadcast([P, TT, 256]),
                                   ALU.mult))
    sig.close()


def merge(M, name, xT, oT, merged, tiles=TT):
    with Stage(M.nc, name) as st:
        sg = st.sb("sg", [P, 2, BANK])
        tmp = st.sb("tmp", [P, 2, BANK])
        t0 = M.weights.taken
        gs, j = [], 0
        for n in range(len(oT)):
            for half in range(2):
                wg = M.weights.view(t0 + 3 * n + 2 * half)
                wb = M.weights.view(t0 + 3 * n + 1)
                cols = slice(half * BANK, (half + 1) * BANK)
                for t in range(tiles):
                    rows = slice(t * P, (t + 1) * P)
                    gs.append(group(
                        lambda pe, bank, wg=wg, rows=rows: matmuls(
                            pe, bank, [(xT[:, k, rows], wg[:, k, :]) for k in range(DK)]),
                        lambda eng, bank, link, j=j: eng.activation(sg[:, j % 2, :], bank, ACT.Sigmoid),
                        "s", t0 + 3 * n + 2 * half, after_v=max(0, j - 1)))

                    def ev(eng, bank, link, j=j, n=n, t=t, cols=cols):
                        if n == 0:
                            return eng.tensor_tensor(merged[:, t, cols], sg[:, j % 2, :], bank, ALU.mult)
                        link(eng.tensor_tensor(tmp[:, j % 2, :], sg[:, j % 2, :], bank, ALU.mult))
                        return eng.tensor_tensor(merged[:, t, cols], merged[:, t, cols], tmp[:, j % 2, :],
                                                 ALU.add)
                    gs.append(group(
                        lambda pe, bank, wb=wb, rows=rows, n=n, cols=cols: matmuls(
                            pe, bank, [(oT[n][:, k, rows], wb[:, k, cols]) for k in range(wb.shape[1])]),
                        ev, "v", t0 + 3 * n + 1, after_s=j + 1))
                    j += 1
        products(M, name + "_p", gs, tiles=3 * len(oT))


def layer_norm(M, name, x, tiles, gain, bias):
    nc = M.nc
    with Stage(nc, name) as st:
        g = st.sb("g", [P, 2, D])
        stats = st.sb("stats", [P, tiles, 2, 6])
        mv = st.sb("mv", [P, tiles, 2])
        rs = st.sb("rs", [P, tiles])
        eps = st.sb("eps", [P, 1])
        sig = st.sig
        with nc.Block() as block:
            @block.sync
            def _(sp):
                sp.dma_start(g[:, 0, :], row_bcast(gain, D)).then_inc(sig["gains"], 16)
                sp.dma_start(g[:, 1, :], row_bcast(bias, D)).then_inc(sig["gains"], 16)

            @block.scalar
            def _(act):
                act.wait_ge(sig["stats"], 1)
                act.activation(rs[:, :], mv[:, :, 1], ACT.Sqrt, bias=eps[:, :]).then_inc(sig["std"], 1)

            @block.vector
            def _(dve):
                link = Chain(dve, sig["chain"])
                link(dve.memset(eps[:, :], LN_EPS))
                for t in range(tiles):
                    for h in range(2):
                        link(dve.bn_stats(stats[:, t, h, :], x[:, t, h * BANK:(h + 1) * BANK]))
                for t in range(tiles):
                    link(dve.bn_aggr(mv[:, t, :], stats[:, t, :, :]))
                dve.sem_inc(sig["stats"], 1)
                dve.wait_ge(sig["std"], 1)
                link(dve.reciprocal(rs[:, :], rs[:, :]))
                dve.wait_ge(sig["gains"], 32)
                for t in range(tiles):
                    link(dve.tensor_scalar(x[:, t, :], x[:, t, :], mv[:, t, 0:1], rs[:, t:t + 1],
                                           ALU.subtract, ALU.mult))
                    link(dve.tensor_tensor(x[:, t, :], x[:, t, :], g[:, 0, :], ALU.mult))
                    link(dve.tensor_tensor(x[:, t, :], x[:, t, :], g[:, 1, :], ALU.add))


def by_rows(dram):
    return dram.rearrange("(t p) d -> p t d", p=P)


def mixer_out(M, merged):
    nc, A = M.nc, M.A
    products(M, "merged_T", transposes(M, lambda t, j: merged[:, t, j * P:(j + 1) * P],
                                       lambda j, a, n: M.xT[:, j, a * P:(a + n) * P], TT, DK))
    with Stage(nc, "wout") as st:
        x = st.sb("x", [P, TT, D])
        t0 = M.weights.taken

        def load(sp):
            sp.dma_start(x[:, :, :], by_rows(A["x"][0])).then_inc(st.sig["x"], 16)

        gs = []
        for half in range(2):
            def ev(eng, bank, link, t, half=half):
                if half == 0 and t == 0:
                    eng.wait_ge(st.sig["x"], 16)
                cols = slice(half * BANK, (half + 1) * BANK)
                return eng.scalar_tensor_tensor(x[:, t, cols], x[:, t, cols], ALPHA, bank, ALU.mult, ALU.add)
            gs += row_groups(M, t0 + half, 0, BANK, M.xT, None, on="v", evac=ev)
        products(M, "wout_p", gs, tiles=2, extra={"sync": load})
        layer_norm(M, "ln1", x, TT, A["ln1_g"][0], A["ln1_b"][0])

        def save(sp):
            sp.dma_start(by_rows(M.x1), x[:, :, :]).then_inc(st.sig["saved"], 16)
            sp.wait_ge(st.sig["saved"], 16)
        products(M, "x1T", transposes(M, lambda t, j: x[:, t, j * P:(j + 1) * P],
                                      lambda j, a, n: M.xT[:, j, a * P:(a + n) * P], TT, DK),
                 extra={"sync": save})


def router(M, route):
    nc, A = M.nc, M.A
    with Stage(nc, "route") as st:
        sig = st.sig
        w = st.sb("w", [P, DK, 36])
        wb = st.sb("wb", [P, 36])
        lg = st.sb("lg", [P, TT, 36])
        iota = st.sb("iota", [P, 32])
        token = st.sb("token", [P, TT], I32)
        strict = st.sb("strict", [P, P])
        nums = st.sb("nums", [1, NBLK])
        zero = st.sb("zero", [P, NBLK * EB // P], I32)
        ge = st.sb("ge", [P, TT, 4])
        gh = st.sb("gh", [P, TT, 4])
        em = st.sb("em", [P, TT, 32])
        tmp = st.sb("tmp", [P, TT, 32])
        hot = st.sb("hot", [P, 3, TT, 32])
        s = st.sb("s", [P, 8, TT])
        cnt = st.sb("cnt", [P, 4, 32])
        le = st.sb("le", [1, NBLK, 32])
        lef = st.sb("lef", [1, NBLK])
        dest_f = st.sb("dest_f", [P, 2, TT])

        def bc(x, n):
            return x.unsqueeze(2).to_broadcast([P, TT, n])

        def rows(x, n):
            return x.unsqueeze(1).to_broadcast([P, TT, n])

        with nc.Block() as block:
            @block.sync
            def _(sp):
                sp.dma_start(w[:, :, 0:4], A["r_group"][0].rearrange("(k p) n -> p k n", p=P)
                             ).then_inc(sig["w"], 16)
                sp.dma_start(w[:, :, 4:36], A["r_expert"][0].rearrange("(k p) n -> p k n", p=P)
                             ).then_inc(sig["w"], 16)
                sp.dma_start(wb[:, 0:4], row_bcast(A["r_group_b"][0], 4)).then_inc(sig["b"], 16)
                sp.dma_start(wb[:, 4:36], row_bcast(A["r_expert_b"][0], 32)).then_inc(sig["b"], 16)

            @block.tensor
            def _(pe):
                pe.wait_ge(sig["w"], 32)
                for t in range(TT):
                    last = matmuls(pe, M.ps[:, 0, t * 36:(t + 1) * 36],
                                   [(M.xT[:, k, t * P:(t + 1) * P], w[:, k, :]) for k in range(DK)])
                last.then_inc(sig["logits"], 1)
                pe.wait_ge(sig["hot"], 1)
                pe.wait_ge(sig["iotas"], 1)
                for t in range(TT):
                    matmuls(pe, M.ps[:, 1, t * 32:(t + 1) * 32],
                            [(M.ones[:, :], hot[:, 2, x, :]) for x in range(t)]
                            + [(strict[:, :], hot[:, 2, t, :])])
                matmuls(pe, M.ps[:, 1, 128:160], [(M.ones[:, :], hot[:, 2, x, :]) for x in range(TT)]
                        ).then_inc(sig["ranks"], 1)

            @block.scalar
            def _(act):
                act.wait_ge(sig["centred"], 1)
                act.activation(ge[:, :, :], ge[:, :, :], ACT.Exp).then_inc(sig["exps"], 1)
                act.wait_ge(sig["gap"], 1)
                act.activation(s[:, 5, :], s[:, 5, :], ACT.Exp).then_inc(sig["exps"], 1)

            @block.gpsimd
            def _(pool):
                link = Chain(pool, sig["made"])
                link(pool.iota(iota[:, :], pattern=[[1, 32]], base=-1000, channel_multiplier=0,
                               allow_small_or_imprecise_dtypes=True))
                link(pool.iota(nums[:, :], pattern=[[1, NBLK]], base=0, channel_multiplier=0,
                               allow_small_or_imprecise_dtypes=True))
                link(pool.iota(token[:, :], pattern=[[P, TT]], base=0, channel_multiplier=1))
                link(pool.memset(zero[:, :], 0))
                link(pool.memset(strict[:, :], 1.0))
                link(pool.affine_select(out=strict[:, :], in_=strict[:, :], compare_op=ALU.is_gt, fill=0.0,
                                        base=0, pattern=[[1, P]], channel_multiplier=-1))
                pool.sem_inc(sig["iotas"], 1)
                pool.dma_start(M.slot_token.rearrange("(p n) o -> p (n o)", p=P), zero[:, :]
                               ).then_inc(sig["slots"], 16)
                pool.wait_ge(sig["slots"], 16)
                pool.wait_ge(sig["dest"], 1)
                for t in range(TT):
                    for c in range(2):
                        pool.indirect_dma_start(
                            out=M.slot_token, out_offset=bass.IndirectOffsetOnAxis(route.dest[:, c, t:t + 1], 0),
                            in_=token[:, t:t + 1], in_offset=None).then_inc(sig["slots"], 16)
                pool.wait_ge(sig["slots"], 16 * 9)

            @block.vector
            def _(dve):
                link = Chain(dve, sig["chain"])

                def one_hot(src, n, top, out, tmp_, least):
                    link(dve.tensor_reduce(top, src, AX, ALU.max))
                    link(dve.tensor_tensor(tmp_, src, bc(top, n), ALU.is_equal))
                    link(dve.tensor_tensor(tmp_, tmp_, rows(iota[:, 0:n], n), ALU.mult))
                    link(dve.tensor_reduce(least, tmp_, AX, ALU.min))
                    link(dve.tensor_tensor(out, rows(iota[:, 0:n], n), bc(least, n), ALU.is_equal))

                dve.wait_ge(sig["logits"], 1)
                dve.wait_ge(sig["b"], 32)
                dve.wait_ge(sig["iotas"], 1)
                link(dve.tensor_tensor(lg[:, :, :], M.ps[:, 0, 0:TT * 36].rearrange("p (t n) -> p t n", n=36),
                                       rows(wb[:, :], 36), ALU.add))
                one_hot(lg[:, :, 0:4], 4, s[:, 0, :], gh[:, :, :], ge[:, :, :], s[:, 1, :])
                dve.tensor_tensor(ge[:, :, :], lg[:, :, 0:4], bc(s[:, 0, :], 4), ALU.subtract
                                  ).then_inc(sig["centred"], 1)
                link(dve.tensor_scalar(gh[:, :, :], gh[:, :, :], -NEG, NEG, ALU.mult, ALU.add))
                for t in range(TT):
                    link(dve.tensor_tensor(em[:, t, :].rearrange("p (g n) -> p g n", n=8),
                                           lg[:, t, 4:36].rearrange("p (g n) -> p g n", n=8),
                                           gh[:, t, :].unsqueeze(2).to_broadcast([P, 4, 8]), ALU.add))
                one_hot(em[:, :, :], 32, s[:, 2, :], hot[:, 0, :, :], tmp[:, :, :], s[:, 1, :])
                link(dve.scalar_tensor_tensor(em[:, :, :], hot[:, 0, :, :], NEG, em[:, :, :],
                                              ALU.mult, ALU.add))
                one_hot(em[:, :, :], 32, s[:, 3, :], hot[:, 1, :, :], tmp[:, :, :], s[:, 1, :])
                dve.tensor_tensor(hot[:, 2, :, :], hot[:, 0, :, :], hot[:, 1, :, :], ALU.add
                                  ).then_inc(sig["hot"], 1)
                dve.tensor_tensor(s[:, 5, :], s[:, 3, :], s[:, 2, :], ALU.subtract).then_inc(sig["gap"], 1)
                dve.wait_ge(sig["exps"], 2)
                link(dve.tensor_reduce(s[:, 6, :], ge[:, :, :], AX, ALU.add))
                link(dve.scalar_tensor_tensor(s[:, 6, :], s[:, 5, :], 1.0, s[:, 6, :], ALU.add, ALU.mult))
                link(dve.reciprocal(route.gate[:, 0, :], s[:, 6, :]))
                link(dve.tensor_tensor(route.gate[:, 1, :], route.gate[:, 0, :], s[:, 5, :], ALU.mult))
                dve.wait_ge(sig["ranks"], 1)
                link(dve.tensor_copy(cnt[:, 0, :], M.ps[:, 1, 128:160]))
                link(dve.tensor_scalar(cnt[:, 1, :], cnt[:, 0, :], 0.0, None, ALU.is_gt))
                for n in range(1, T // EB):
                    link(dve.scalar_tensor_tensor(cnt[:, 1, :], cnt[:, 0, :], float(n * EB), cnt[:, 1, :],
                                                  ALU.is_gt, ALU.add))
                link(dve.memset(cnt[:, 3, :], 1.0))
                link(dve.tensor_tensor_scan(cnt[:, 2, :], cnt[:, 3, :], cnt[:, 1, :], 0.0, ALU.mult, ALU.add))
                link(dve.tensor_tensor(cnt[:, 3, :], cnt[:, 2, :], cnt[:, 1, :], ALU.subtract))
                link(dve.tensor_scalar(cnt[:, 3, :], cnt[:, 3, :], float(EB), None, ALU.mult))
                link(dve.tensor_tensor(tmp[:, :, :], M.ps[:, 1, 0:128].rearrange("p (t n) -> p t n", n=32),
                                       rows(cnt[:, 3, :], 32), ALU.add))
                for c in range(2):
                    link(dve.tensor_tensor(em[:, :, :], tmp[:, :, :], hot[:, c, :, :], ALU.mult))
                    link(dve.tensor_reduce(dest_f[:, c, :], em[:, :, :], AX, ALU.add))
                link(dve.tensor_copy(route.dest[:, :, :], dest_f[:, :, :]))
                dve.sem_inc(sig["dest"], 1)
                link(dve.tensor_tensor(le[:, :, :], cnt[0:1, 2, :].unsqueeze(1).to_broadcast([1, NBLK, 32]),
                                       nums[:, :].unsqueeze(2).to_broadcast([1, NBLK, 32]), ALU.is_le))
                link(dve.tensor_reduce(lef[:, :], le[:, :, :], AX, ALU.add))
                link(dve.tensor_scalar(route.expert[:, 0:NBLK], lef[:, :], 31.0, None, ALU.min))
                link(dve.tensor_copy(route.expert[:, NBLK:NBLK + 1], cnt[0:1, 2, 31:32]))
                link(dve.tensor_tensor(le[:, 0:NBLK // 2, 0], nums[:, :].rearrange("o (n t) -> o n t", t=2)[:, :, 0],
                                       cnt[0:1, 2, 31:32].to_broadcast([1, NBLK // 2]), ALU.is_lt))
                link(dve.tensor_reduce(lef[:, 0:1], le[:, 0:NBLK // 2, 0], AX, ALU.add))
                link(dve.tensor_copy(route.expert[:, NBLK + 1:NBLK + 2], lef[:, 0:1]))


EB = 128
NE = 32
NBLK = (2 * T + NE * (EB - 1)) // EB
NBLK += NBLK % 2
FF = 512


def experts(M, route):
    nc, A = M.nc, M.A
    ds = bass.ds
    steps_max = NBLK // 2
    with Stage(nc, "moe") as st:
        sig = st.sig
        wg, wu, wd = [st.sb(n, [P, 2, TILE]) for n in ("wg", "wu", "wd")]
        idx = st.sb("idx", [P, NBLK + 2], I32)
        xg = st.sb("xg", [P, 2, D])
        xgT = st.sb("xgT", [P, 2, DK, P])
        sg = st.sb("sg", [P, 2, FF])
        h = st.sb("h", [P, 2, FF])
        hT = st.sb("hT", [P, 2, FF])
        y = st.sb("y", [P, 2, D])
        done = st.sb("done", [1, 1])
        x_ps = M.ps[:, 0:2, :].rearrange("p b n -> p (b n)")
        g_ps, u_ps, h_ps = M.ps[:, 2, :], M.ps[:, 3, :], M.ps[:, 4, :]
        y_ps = M.ps[:, 5:7, :].rearrange("p b n -> p (b n)")

        def steps(eng, body):
            used = eng.value_load(route.expert[0:1, NBLK:NBLK + 1], min_val=1, max_val=NBLK)
            with eng.Fori(0, steps_max) as i:
                with eng.If(i * 2 < used):
                    body(i)

        with nc.Block() as block:
            @block.sync
            def _(sp):
                def body(i):
                    for j in range(2):
                        n = i * 2 + j
                        e = sp.value_load(route.expert[0:1, ds(n, 1)], min_val=0, max_val=NE - 1)
                        for name, buf, w in (("g", wg, "e_gate"), ("u", wu, "e_up")):
                            sp.wait_ge(sig[f"{name}_done"], n + 1)
                            sp.dma_start(buf[:, j, :].rearrange("p (k n) -> p k n", n=FF),
                                         A[w][0, ds(e, 1)].rearrange("o (k p) n -> p (o k) n", p=P)
                                         ).then_inc(sig[f"{name}_in{j}"], 16)
                        sp.wait_ge(sig["d_done"], n + 1)
                        sp.dma_start(wd[:, j, :].rearrange("p (k n) -> p k n", n=D),
                                     A["e_down"][0, ds(e, 1)].rearrange("o (k p) n -> p (o k) n", p=P)
                                     ).then_inc(sig[f"d_in{j}"], 16)
                steps(sp, body)

            @block.gpsimd
            def _(pool):
                for n in range(NBLK + 2):
                    b = n % NBLK
                    pool.dma_start(idx[:, n:n + 1], M.slot_token[b * P:(b + 1) * P, :]
                                   ).then_inc(sig["idx"], 16)
                pool.wait_ge(sig["idx"], 16 * (NBLK + 2))

                def gather(n):
                    if n >= 2:
                        pool.wait_ge(sig["x_turned"], n + 1)
                    pool.indirect_dma_start(
                        out=xg[:, n % 2, :], out_offset=None, in_=M.x1,
                        in_offset=bass.IndirectOffsetOnAxis(idx[:, n:n + 1], 0)
                    ).then_inc(sig[f"x_in{n % 2}"], 16)
                gather(0)
                gather(1)
                used = pool.value_load(route.expert[0:1, NBLK:NBLK + 1], min_val=1, max_val=NBLK)
                for i in range(steps_max):
                    with pool.If(used > 2 * i):
                        gather(2 * i + 2)
                        gather(2 * i + 3)

            @block.tensor
            def _(pe):
                def product(out, left, w, chunks, done_):
                    for half in range(w.shape[2] // BANK):
                        last = matmuls(pe, out[:, half * BANK:(half + 1) * BANK],
                                       [(left(k), w[:, k, half * BANK:(half + 1) * BANK]) for k in range(chunks)])
                    last.then_inc(sig[done_], 1)

                def turn(i, j, n, arrived):
                    pe.wait_ge(sig[f"x_in{j}"], arrived)
                    pe.wait_ge(sig["x_moved"], n + 2)
                    for k in range(DK):
                        last = pe.transpose(x_ps[:, k * P:(k + 1) * P], xg[:, j, k * P:(k + 1) * P],
                                            M.ident[:, :])
                    last.then_inc(sig["x_turned"], 1)

                def gate(i, j, n):
                    pe.wait_ge(sig[f"g_in{j}"], (i + 1) * 16)
                    pe.wait_ge(sig["x_moved"], n + 3)
                    pe.wait_ge(sig["silus"], n + 2)
                    product(g_ps, lambda k: xgT[:, j, k, :],
                            wg[:, j, :].rearrange("p (k n) -> p k n", n=FF), DK, "g_done")

                def up(i, j, n):
                    pe.wait_ge(sig[f"u_in{j}"], (i + 1) * 16)
                    pe.wait_ge(sig["h"], n + 2)
                    product(u_ps, lambda k: xgT[:, j, k, :],
                            wu[:, j, :].rearrange("p (k n) -> p k n", n=FF), DK, "u_done")

                def turn_h(i, j, n):
                    pe.wait_ge(sig["h"], n + 3)
                    pe.wait_ge(sig["h_moved"], n + 2)
                    for f in range(FF // P):
                        last = pe.transpose(h_ps[:, f * P:(f + 1) * P], h[:, j, f * P:(f + 1) * P],
                                            M.ident[:, :])
                    last.then_inc(sig["h_turned"], 1)

                def down(i, j, n):
                    pe.wait_ge(sig[f"d_in{j}"], (i + 1) * 16)
                    pe.wait_ge(sig["h_moved"], n + 3)
                    pe.wait_ge(sig["y"], n + 2)
                    product(y_ps, lambda f: hT[:, j, f * P:(f + 1) * P],
                            wd[:, j, :].rearrange("p (k n) -> p k n", n=D), FF // P, "d_done")

                def body(i):
                    n = i * 2
                    gate(i, 0, n)
                    up(i, 0, n)
                    gate(i, 1, n + 1)
                    turn_h(i, 0, n)
                    up(i, 1, n + 1)
                    down(i, 0, n)
                    turn(i + 1, 0, n + 2, (i + 2) * 16)
                    turn_h(i, 1, n + 1)
                    down(i, 1, n + 1)
                    turn(i + 1, 1, n + 3, (i + 2) * 16)

                for name in ("x_turned", "g_done", "u_done", "h_turned", "d_done"):
                    pe.sem_inc(sig[name], 2)
                turn(0, 0, 0, 16)
                turn(0, 1, 1, 16)
                steps(pe, body)

            @block.scalar
            def _(act):
                def silu(i, j, n):
                    act.wait_ge(sig["g_done"], n + 3)
                    act.wait_ge(sig["h"], n + 1)
                    act.activation(sg[:, j, :], g_ps, ACT.Silu).then_inc(sig["silus"], 1)

                def move_h(i, j, n):
                    act.wait_ge(sig["h_turned"], n + 3)
                    act.wait_ge(sig["d_done"], n + 1)
                    act.activation(hT[:, j, :], h_ps, ACT.Copy).then_inc(sig["h_moved"], 1)

                def out(i, j, n):
                    act.wait_ge(sig["d_done"], n + 3)
                    act.wait_ge(sig[f"y_out{j}"], (i + 1) * 16)
                    act.activation(y[:, j, :], y_ps, ACT.Copy).then_inc(sig["y"], 1)
                    act.wait_ge(sig["y"], n + 3)
                    act.dma_start(M.y_slot[ds(n * P, P), :], y[:, j, :]).then_inc(sig[f"y_out{j}"], 16)

                def body(i):
                    n = i * 2
                    silu(i, 0, n)
                    silu(i, 1, n + 1)
                    move_h(i, 0, n)
                    out(i, 0, n)
                    move_h(i, 1, n + 1)
                    out(i, 1, n + 1)

                for name, n in (("silus", 2), ("h_moved", 2), ("y", 2), ("y_out0", 16), ("y_out1", 16)):
                    act.sem_inc(sig[name], n)
                steps(act, body)
                taken = act.value_load(route.expert[0:1, NBLK + 1:NBLK + 2], min_val=1, max_val=steps_max)
                act.wait_ge(sig["y_out0"], (taken + 1) * 16)
                act.wait_ge(sig["y_out1"], (taken + 1) * 16)
                act.activation(done[:, :], M.ident[0:1, 0:1], ACT.Copy).then_inc(sig["done"], 1)

            @block.vector
            def _(dve):
                def move_x(j, n):
                    dve.wait_ge(sig["x_turned"], n + 3)
                    dve.wait_ge(sig["u_done"], n + 1)
                    dve.tensor_copy(xgT[:, j, :, :].rearrange("p m n -> p (m n)"), x_ps
                                    ).then_inc(sig["x_moved"], 1)

                def multiply(j, n):
                    dve.wait_ge(sig["silus"], n + 3)
                    dve.wait_ge(sig["u_done"], n + 3)
                    dve.wait_ge(sig["h_turned"], n + 1)
                    dve.tensor_tensor(h[:, j, :], sg[:, j, :], u_ps, ALU.mult).then_inc(sig["h"], 1)

                def body(i):
                    n = i * 2
                    multiply(0, n)
                    multiply(1, n + 1)
                    move_x(0, n + 2)
                    move_x(1, n + 3)
                dve.sem_inc(sig["x_moved"], 2)
                dve.sem_inc(sig["h"], 2)
                move_x(0, 0)
                move_x(1, 1)
                steps(dve, body)


def combine(M, route):
    nc, A = M.nc, M.A
    with Stage(nc, "comb") as st:
        sig = st.sig
        x = st.sb("x", [P, TT, D])
        yg = st.sb("yg", [P, 2, TT, D])
        with nc.Block() as block:
            @block.sync
            def _(sp):
                sp.dma_start(x[:, :, :], by_rows(M.x1)).then_inc(sig["x"], 16)

            @block.gpsimd
            def _(pool):
                for t in range(TT):
                    for c in range(2):
                        pool.indirect_dma_start(
                            out=yg[:, c, t, :], out_offset=None, in_=M.y_slot,
                            in_offset=bass.IndirectOffsetOnAxis(route.dest[:, c, t:t + 1], 0)
                        ).then_inc(sig[f"y{t}"], 16)

            @block.vector
            def _(dve):
                link = Chain(dve, sig["chain"])
                dve.wait_ge(sig["x"], 16)
                for t in range(TT):
                    link(dve.tensor_scalar(x[:, t, :], x[:, t, :], ALPHA, None, ALU.mult))
                    dve.wait_ge(sig[f"y{t}"], 32)
                    for c in range(2):
                        link(dve.scalar_tensor_tensor(x[:, t, :], yg[:, c, t, :], route.gate[:, c, t:t + 1],
                                                      x[:, t, :], ALU.mult, ALU.add))
        layer_norm(M, "ln2", x, TT, A["ln2_g"][0], A["ln2_b"][0])
        with nc.Block() as block:
            @block.sync
            def _(sp):
                sp.dma_start(by_rows(M.x_lat), x[:, :, :]).then_inc(sig["saved"], 16)
                sp.wait_ge(sig["saved"], 16)



CTX = 256
TA = (T + CTX) // P
MH, QK, NOPE, ROPE = 8, 96, 64, 32
Q_LORA, KV_LORA = 768, 256
OFF_CQ = 2 * D
OFF_CKV = OFF_CQ + Q_LORA
OFF_NA = OFF_CKV + KV_LORA + ROPE
NA_W = 512
DFF = 4 * D
GRID_W, ROWS = 64, 8
EPS = 1e-6
RPB_H, RPB_W = 15, 31
LAYERS = 2


def second_tiles(A):
    tiles = []
    for l in range(LAYERS):
        w = A["w_in_2"][l]
        tiles += weight_tiles(A["w_ada_2"][l], 0, 6 * D)
        tiles += weight_tiles(w, OFF_CQ, OFF_CKV)
        tiles += weight_tiles(A["w_uq_2"][l], 0, MH * QK)
        tiles += weight_tiles(w, OFF_CKV, OFF_NA)
        tiles += weight_tiles(A["w_ukv_2"][l], 0, MH * 2 * HD, D)
        tiles += weight_tiles(w, OFF_NA, OFF_NA + 3 * NA_W)
        for n, o in enumerate(("w_mla_o_2", "w_na_o_2")):
            g = weight_tiles(w, n * D, (n + 1) * D)
            tiles += [g[0]] + weight_tiles(A[o][l], 0, D, D) + [g[1]]
        tiles += weight_tiles(A["w_out_2"][l], 0, D)
        tiles += weight_tiles(A["w_ff1_2"][l], 0, DFF)
        for half in range(2):
            for k in range(4):
                tiles += weight_tiles(A["w_ff2_2"][l, k * D:(k + 1) * D], half * BANK, (half + 1) * BANK)
    return tiles


def rms_rows(M, name, x, tiles, heads, d, gain=None, rope=None, load=None, sq=None):
    nc = M.nc
    with Stage(nc, name) as st:
        sig = st.sig
        slots = 1 if sq is not None else 2
        if sq is None:
            sq = st.sb("sq", [P, 2, heads * d])
        ss = st.sb("ss", [P, tiles, heads])
        rs = st.sb("rs", [P, tiles, heads])
        eps = st.sb("eps", [P, 1])
        if rope is not None:
            tmp = st.sb("tmp", [P, 4, heads, 8])

        def heads_of(v):
            return v.rearrange("p (h n) -> p h n", n=d)

        with nc.Block() as block:
            if load:
                @block.sync
                def _(sp):
                    for t in range(tiles):
                        load(sp, t).then_inc(sig[f"in{t}"], 16)

            @block.scalar
            def _(act):
                def root(t):
                    act.wait_ge(sig["summed"], t + 1)
                    act.activation(rs[:, t, :], ss[:, t, :], ACT.Sqrt, bias=eps[:, :], scale=1.0 / d
                                   ).then_inc(sig["root"], 1)
                act.wait_ge(sig["eps"], 1)
                for t in range(tiles):
                    if load:
                        act.wait_ge(sig[f"in{t}"], 16)
                    if t >= slots:
                        act.wait_ge(sig["summed"], t - slots + 1)
                    if heads == 1:
                        act.activation(sq[:, t % slots, :], x[:, t, :], ACT.Square, accum_out=ss[:, t, :]
                                       ).then_inc(sig["squared"], 1)
                    else:
                        act.activation(sq[:, t % slots, :], x[:, t, :], ACT.Square).then_inc(sig["squared"], 1)
                    if t >= 1:
                        root(t - 1)
                root(tiles - 1)

            @block.vector
            def _(dve):
                link = Chain(dve, sig["chain"])
                dve.memset(eps[:, :], EPS).then_inc(sig["eps"], 1)

                def scale(t):
                    dve.wait_ge(sig["root"], t + 1)
                    link(dve.reciprocal(rs[:, t, :], rs[:, t, :]))
                    if heads == 1:
                        link(dve.tensor_scalar(x[:, t, :], x[:, t, :], rs[:, t, :], None, ALU.mult))
                    else:
                        xh = heads_of(x[:, t, :])
                        link(dve.tensor_tensor(xh, xh, rs[:, t, :].unsqueeze(2).to_broadcast([P, heads, d]),
                                               ALU.mult))
                        if gain is not None:
                            link(dve.tensor_tensor(xh, xh, gain.unsqueeze(1).to_broadcast([P, heads, d]),
                                                   ALU.mult))
                    if rope is not None and t < TT:
                        for half in range(2):
                            x1, x2 = (heads_of(x[:, t, :])[:, :, NOPE + 16 * half + 8 * i:
                                                           NOPE + 16 * half + 8 * (i + 1)] for i in range(2))
                            cos, sin = (rope[:, i, t, half, :].unsqueeze(1).to_broadcast([P, heads, 8])
                                        for i in range(2))
                            for i, (a, b) in enumerate(((x1, cos), (x2, sin), (x1, sin), (x2, cos))):
                                (link if i == 3 else link.post)(
                                    dve.tensor_tensor(tmp[:, i, :, :], a, b, ALU.mult))
                            link.post(dve.tensor_tensor(x1, tmp[:, 0, :, :], tmp[:, 1, :, :],
                                                        ALU.subtract))
                            link(dve.tensor_tensor(x2, tmp[:, 2, :, :], tmp[:, 3, :, :],
                                                   ALU.add))

                for t in range(tiles):
                    dve.wait_ge(sig["squared"], t + 1)
                    if heads == 1:
                        dve.sem_inc(sig["summed"], 1)
                    else:
                        dve.tensor_reduce(ss[:, t, :], heads_of(sq[:, t % slots, :]), AX, ALU.add
                                          ).then_inc(sig["summed"], 1)
                    if t >= 1:
                        scale(t - 1)
                scale(tiles - 1)


def scaled(eng, out, in_, scale, bias=None):
    if on_scalar(eng):
        if bias is None:
            return eng.activation(out, in_, ACT.Copy, scale=scale)
        return eng.activation(out, in_, ACT.Identity, scale=scale, bias=bias)
    if bias is None:
        return eng.tensor_scalar(out, in_, scale, None, ALU.mult)
    return eng.tensor_scalar(out, in_, scale, bias, ALU.mult, ALU.add)


def ada(M, L, l):
    nc, A = M.nc, M.A
    with Stage(nc, f"ada{l}") as st:
        sig = st.sig
        c = st.sb("c", [P, 2, DK])
        cs = st.sb("cs", [P, DK, 2])
        b = st.sb("b", [P, 6 * DK])
        g = st.sb("g", [P, 2, DK])
        with nc.Block() as block:
            @block.sync
            def _(sp):
                sp.dma_start(c[:, 0, :], A["c_2"]).then_inc(sig["in"], 16)
                sp.dma_start(c[:, 1, :], A["c_ctx_2"]).then_inc(sig["in"], 16)
                sp.dma_start(b[:, :], A["b_ada_2"][l]).then_inc(sig["small"], 16)
                sp.dma_start(g[:, 0, :], A["g_attn_2"][l]).then_inc(sig["small"], 16)
                sp.dma_start(g[:, 1, :], A["g_mlp_2"][l]).then_inc(sig["small"], 16)
                sp.wait_ge(sig["small"], 48)

            @block.scalar
            def _(act):
                act.wait_ge(sig["in"], 32)
                act.activation(cs[:, :, :].rearrange("p k s -> p s k"), c[:, :, :], ACT.Silu
                               ).then_inc(sig["silu"], 1)
                act.wait_ge(sig["silu"], 1)
        rows = st.sb("rows", [2, 6 * D])
        gs, t0 = [], M.weights.taken
        for i in range(12):
            w = M.weights.view(t0 + i)
            gs.append(group(
                lambda pe, bank, w=w: matmuls(pe, bank[0:2, :], [(cs[:, k, :], w[:, k, :]) for k in range(DK)]),
                lambda eng, bank, link, i=i: move(eng, rows[:, i * BANK:(i + 1) * BANK], bank[0:2, :]),
                "v", t0 + i))

        def turn(pe, bank):
            for c in range(6 * DK):
                last = pe.transpose(bank[:, 2 * c:2 * c + 2], rows[:, c * P:(c + 1) * P], M.ident[0:2, 0:2])
            return last

        def add_bias(eng, bank, link):
            return eng.tensor_tensor(L.mod[:, :, :], bank[:, 0:12 * DK].rearrange("p (c s) -> p c s", s=2),
                                     b[:, :].unsqueeze(2).to_broadcast([P, 6 * DK, 2]), ALU.add)
        products(M, f"ada_p{l}", gs, tiles=12)
        products(M, f"ada_t{l}", [group(turn, add_bias, "v")])
        with nc.Block() as block:
            @block.vector
            def _(dve):
                for n, gain in ((0, L.gain1), (1, L.gain2)):
                    sc = L.mod[:, (3 * n + 1) * DK:(3 * n + 2) * DK, :]
                    dve.scalar_tensor_tensor(gain[:, :, :], sc, 1.0,
                                             g[:, n, :].unsqueeze(2).to_broadcast([P, DK, 2]),
                                             ALU.add, ALU.mult).then_inc(sig["gains"], 1)
                dve.wait_ge(sig["gains"], 2)


def gate_rows(M, name, mod, chunk, streams, out):
    gs = []
    for s in range(streams):
        for half in range(2):
            def pe(pe_, bank, s=s, half=half):
                for x in range(4):
                    c = chunk + 4 * half + x
                    last = pe_.matmul(bank[:, x * P:(x + 1) * P], mod[:, c, s:s + 1].to_broadcast([P, P]),
                                      M.ident[:, :], start=True, stop=True)
                return last
            gs.append(group(pe, lambda eng, bank, link, s=s, half=half:
                            move(eng, out[:, s, half * BANK:(half + 1) * BANK], bank), "vs"[half]))
    products(M, name, gs)


def modulated(M, L, name, tiles, x, gain, shift, hT):
    def ev(eng, bank, link, j, t0, n):
        s = 0 if t0 < TT else 1
        return scaled(eng, hT[:, j, t0 * P:(t0 + n) * P], bank, gain[:, j, s:s + 1],
                      L.mod[:, shift + j, s:s + 1])
    products(M, name, transposes(M, lambda t, j: x[:, t, j * P:(j + 1) * P], None, tiles, DK, evac=ev))


def head_transposes(M, x, dst, tiles, scale=None):
    gs = []
    for h in range(MH):
        for t0 in range(0, tiles, 4):
            n = min(4, tiles - t0)

            def pe(pe_, bank, h=h, t0=t0, n=n):
                for t in range(n):
                    last = pe_.transpose(bank[0:QK, t * P:(t + 1) * P], x[:, t0 + t, h * QK:(h + 1) * QK],
                                         M.ident[:, :])
                return last
            gs.append(group(pe, lambda eng, bank, link, h=h, t0=t0, n=n: move(
                eng, dst[:, h, t0 * P:(t0 + n) * P], bank[0:QK, 0:n * P], scale), "vs"[len(gs) % 2]))
    return gs


def latent_attention(M, L, l, hT, yT):
    nc, A, tq = M.nc, M.A, L.tq
    with Stage(nc, f"mla{l}") as st:
        qT = st.sb("qT", [QK, MH, tq * P])
        kT = st.sb("kT", [QK, MH, TA * P])
        v = st.sb("v", [P, TA, MH * HD])
        with Stage(nc, f"mla_in{l}") as si:
            rope = si.sb("rope", [P, 2, TT, 2, 8])
            gains = si.sb("gains", [P, 2, QK])
            g_col = si.sb("g_col", [P, 8])
            with Stage(nc, f"mla_q{l}") as sq:
                q = sq.sb("q", [P, tq, Q_LORA])
                cqT = sq.sb("cqT", [P, Q_LORA // P, tq * P])
                t0 = M.weights.taken

                def small(sp):
                    s = si.sig["small"]
                    sp.dma_start(rope[:, 0, :, :, :], A["rope_cos"]).then_inc(s, 16)
                    sp.dma_start(rope[:, 1, :, :, :], A["rope_sin"]).then_inc(s, 16)
                    sp.dma_start(gains[:, 0, :], row_bcast(A["g_mla_q_2"][l], QK)).then_inc(s, 16)
                    sp.dma_start(gains[:, 1, :], row_bcast(A["g_mla_k_2"][l], QK)).then_inc(s, 16)
                    sp.dma_start(g_col[:, 0:6], A["g_qa_2"][l]).then_inc(s, 16)
                    sp.dma_start(g_col[:, 6:8], A["g_kva_2"][l]).then_inc(s, 16)
                    sp.wait_ge(s, 6 * 16)
                gs = []
                for c, w in ((0, BANK), (BANK, 256)):
                    gs += row_groups(M, t0 + c // BANK, 0, w, hT, lambda t, c=c, w=w: q[:, t, c:c + w],
                                     rows=tq * P)
                products(M, f"cq{l}", gs, tiles=2, extra={"sync": small})
                rms_rows(M, f"cq_norm{l}", q, tq, 1, Q_LORA)
                products(M, f"cqT{l}", transposes(
                    M, lambda t, j: q[:, t, j * P:(j + 1) * P], None, tq, 6,
                    evac=lambda eng, bank, link, j, a, n: scaled(eng, cqT[:, j, a * P:(a + n) * P], bank,
                                                                 g_col[:, j:j + 1])))
                gs = []
                for c, w in ((0, BANK), (BANK, 256)):
                    gs += row_groups(M, t0 + 2 + c // BANK, 0, w, cqT, lambda t, c=c, w=w: q[:, t, c:c + w],
                                     rows=tq * P)
                products(M, f"q{l}", gs, tiles=2)
                rms_rows(M, f"q_norm{l}", q, tq, MH, QK, gains[:, 0, :], rope)
                products(M, f"qT{l}", head_transposes(M, q, qT, tq, QK ** -0.5))
            with Stage(nc, f"mla_k{l}") as sk:
                ckv = sk.sb("ckv", [P, TA, KV_LORA])
                k_r = sk.sb("k_r", [P, TA, ROPE])
                ckvT = sk.sb("ckvT", [P, 2, TA * P])
                k = sk.sb("k", [P, TA, MH * QK])
                t0 = M.weights.taken
                products(M, f"ckv{l}",
                         row_groups(M, t0, 0, KV_LORA, hT, lambda t: ckv[:, t, :], rows=TA * P)
                         + row_groups(M, t0, KV_LORA, ROPE, hT, lambda t: k_r[:, t, :], rows=TA * P), tiles=1)
                rms_rows(M, f"ckv_norm{l}", ckv, TA, 1, KV_LORA)
                products(M, f"ckvT{l}", transposes(
                    M, lambda t, j: ckv[:, t, j * P:(j + 1) * P], None, TA, 2,
                    evac=lambda eng, bank, link, j, a, n: scaled(eng, ckvT[:, j, a * P:(a + n) * P], bank,
                                                                 g_col[:, 6 + j:7 + j])))
                gs = []
                for half in range(2):
                    def ev(eng, bank, link, t, half=half):
                        b = bank.rearrange("p (h x n) -> p h x n", h=4, n=HD)
                        kh = k[:, t, half * 4 * QK:(half + 1) * 4 * QK].rearrange("p (h n) -> p h n", n=QK)
                        vh = v[:, t, half * 4 * HD:(half + 1) * 4 * HD].rearrange("p (h n) -> p h n", n=HD)
                        link(move(eng, kh[:, :, 0:NOPE], b[:, :, 0, :]))
                        link(move(eng, kh[:, :, NOPE:QK], k_r[:, t, :].unsqueeze(1).to_broadcast([P, 4, ROPE])))
                        return move(eng, vh, b[:, :, 1, :])
                    gs += row_groups(M, t0 + 1, half * BANK, BANK, ckvT, None, rows=TA * P, evac=ev)
                products(M, f"kv{l}", gs, tiles=1)
                rms_rows(M, f"k_norm{l}", k, TA, MH, QK, gains[:, 1, :], rope)
                products(M, f"kT{l}", head_transposes(M, k, kT, TA))
        o = st.sb("o", [P, tq, MH * HD])
        units = []
        for h in range(MH):
            for t in range(tq):
                q_t = qT[:, h, t * P:(t + 1) * P]
                if t < TT:
                    segs = [(q_t, kT[:, h, 0:T], T, None), (q_t, kT[:, h, T:T + CTX], CTX, None)]
                    keys = range(TA)
                else:
                    segs = [(q_t, kT[:, h, T:T + CTX], CTX, None)]
                    keys = range(TT, TA)
                units.append(Unit(segs=segs, pv=[v[:, s, h * HD:(h + 1) * HD] for s in keys],
                                             out=o[:, t, h * HD:(h + 1) * HD]))
        attention(M, st, units, 2, T + CTX, False)
        products(M, f"mla_oT{l}", transposes(M, lambda t, j: o[:, t, j * P:(j + 1) * P],
                                             lambda j, a, n: yT[:, j, a * P:(a + n) * P], tq, 4))


def bias_tables(M, st, l, h0, heads, table, column_mask, flip):
    nc = M.nc
    rev = st.sb("rev", [P, 2, RPB_H * GRID_W])
    parts = ((0, 8), (8, RPB_H))
    sig = Signals(nc, f"bias{l}_{h0}")
    with nc.Block() as block:
        @block.sync
        def _(sp):
            for i in range(heads):
                if i >= 2:
                    sp.wait_ge(sig["flipped"], 2 * (i - 1))
                for b in range(2):
                    off = 2 * GRID_W + (h0 + i) * RPB_H * RPB_W - b * RPB_W + RPB_W // 2 - (GRID_W - 1)
                    sp.dma_start(rev[b * GRID_W:(b + 1) * GRID_W, i % 2, :].rearrange("p (a c) -> p a c", c=GRID_W),
                                 bass.AP(M.rpb_pad.tensor, off, [[1, GRID_W], [RPB_W, RPB_H], [1, GRID_W]])
                                 ).then_inc(sig[f"in{i}"], 16)

        @block.tensor
        def _(pe):
            for i in range(heads):
                pe.wait_ge(sig[f"in{i}"], 32)
                for j, (a0, a1) in enumerate(parts):
                    pe.matmul(M.ps[:, 2 * i + j, 0:(a1 - a0) * GRID_W], flip[:, :],
                              rev[:, i % 2, a0 * GRID_W:a1 * GRID_W], start=True, stop=True
                              ).then_inc(sig["flipped"], 1)

        @block.vector
        def _(dve):
            for i in range(heads):
                for j, (a0, a1) in enumerate(parts):
                    dve.wait_ge(sig["flipped"], 2 * i + j + 1)
                    n = a1 - a0
                    dve.tensor_tensor(
                        table[:, i, a0 * GRID_W:a1 * GRID_W].rearrange("p (a c) -> p a c", c=GRID_W),
                        M.ps[:, 2 * i + j, 0:n * GRID_W].rearrange("p (a c) -> p a c", c=GRID_W),
                        column_mask[:, :].unsqueeze(1).to_broadcast([P, n, GRID_W]), ALU.add
                    ).then_inc(sig["masked"], 1)
            dve.wait_ge(sig["masked"], 2 * heads)
    sig.close()


def pad_bias(M, l):
    nc, A = M.nc, M.A
    n = MH * RPB_H * RPB_W
    with Stage(nc, f"pad{l}") as st:
        z = st.sb("z", [1, 2 * GRID_W])
        sig = st.sig
        with nc.Block() as block:
            @block.vector
            def _(dve):
                dve.memset(z[:, :], 0.0).then_inc(sig["zero"], 1)

            @block.sync
            def _(sp):
                flat = M.rpb_pad.rearrange("n -> () n")
                sp.dma_start(flat[:, 2 * GRID_W:2 * GRID_W + n], A["rpb_2"][l].rearrange("h a b -> () (h a b)")
                             ).then_inc(sig["out"], 16)
                sp.wait_ge(sig["zero"], 1)
                sp.dma_start(flat[:, 0:2 * GRID_W], z[:, :]).then_inc(sig["out"], 16)
                sp.dma_start(flat[:, 2 * GRID_W + n:], z[:, 0:GRID_W]).then_inc(sig["out"], 16)
                sp.wait_ge(sig["out"], 48)


def neighbourhood_attention(M, L, l, hT, yT):
    nc, A, tq = M.nc, M.A, L.tq
    with Stage(nc, f"na{l}") as st:
        qT = st.sb("qT", [P, 4, tq * P])
        kT = st.sb("kT", [P, 4, TA * P])
        v = st.sb("v", [P, TA, NA_W])
        column_mask = st.sb("column_mask", [P, GRID_W])
        zero = st.sb("zero", [P, CTX])
        flip = st.sb("flip", [P, P])
        with Stage(nc, f"na_in{l}") as si:
            q = si.sb("q", [P, tq, NA_W])
            k = si.sb("k", [P, TA, NA_W])
            gains = si.sb("gains", [P, 2, HD])

            def masks(pool):
                link = Chain(pool, si.sig["masks"])
                link(pool.memset(zero[:, :], 0.0))
                link(pool.memset(column_mask[:, :], 0.0))
                link(pool.memset(flip[:, :], 0.0))
                for b in range(2):
                    link(pool.affine_select(out=flip[:, :], in_=flip[:, :], compare_op=ALU.not_equal,
                                            fill=1.0, base=-(2 * b * GRID_W + GRID_W - 1),
                                            pattern=[[1, P]], channel_multiplier=1))
                for p0 in (0, HD):
                    m = column_mask[p0:p0 + HD, :]
                    link(pool.affine_select(out=m[:, 0:48], in_=m[:, 0:48], compare_op=ALU.is_ge, fill=NEG,
                                            base=8, pattern=[[1, 48]], channel_multiplier=-1))
                    link(pool.affine_select(out=m[:, 16:64], in_=m[:, 16:64], compare_op=ALU.is_ge, fill=NEG,
                                            base=7 - 16, pattern=[[-1, 48]], channel_multiplier=1))

            def small(sp):
                s = si.sig["small"]
                sp.dma_start(gains[:, 0, :], row_bcast(A["g_na_q_2"][l], HD)).then_inc(s, 16)
                sp.dma_start(gains[:, 1, :], row_bcast(A["g_na_k_2"][l], HD)).then_inc(s, 16)
                sp.wait_ge(s, 32)
            t0 = M.weights.taken
            products(M, f"na_p{l}",
                     row_groups(M, t0, 0, NA_W, hT, lambda t: q[:, t, :], rows=tq * P)
                     + row_groups(M, t0 + 1, 0, NA_W, hT, lambda t: k[:, t, :], rows=TA * P)
                     + row_groups(M, t0 + 2, 0, NA_W, hT, lambda t: v[:, t, :], rows=TA * P),
                     tiles=3, extra={"sync": small, "gpsimd": masks})
            rms_rows(M, f"nq_norm{l}", q, tq, MH, HD, gains[:, 0, :])
            rms_rows(M, f"nk_norm{l}", k, TA, MH, HD, gains[:, 1, :])
            products(M, f"na_qT{l}",
                     transposes(M, lambda t, j: q[:, t, j * P:(j + 1) * P], None, tq, 4,
                                evac=lambda eng, bank, link, j, a, n: move(
                                    eng, qT[:, j, a * P:(a + n) * P], bank, HD ** -0.5))
                     + transposes(M, lambda t, j: k[:, t, j * P:(j + 1) * P],
                                  lambda j, a, n: kT[:, j, a * P:(a + n) * P], TA, 4))
        o = st.sb("o", [P, tq, NA_W])
        pad_bias(M, l)
        for h0 in (0, 4):
            with Stage(nc, f"na_att{l}_{h0}") as sa:
                table = sa.sb("table", [P, 4, RPB_H * GRID_W])
                bias_tables(M, sa, l, h0, 4, table, column_mask, flip)
                units = []
                for h in range(h0, h0 + 4):
                    hp, hc = (h % 2) * HD, h // 2
                    for t in range(tq):
                        q_t = qT[hp:hp + HD, hc, t * P:(t + 1) * P]
                        segs = [(q_t, kT[hp:hp + HD, hc, T:T + CTX], CTX, zero[:, :])]
                        keys = list(range(TT, TA))
                        if t < TT:
                            a = (ROWS - 1 - 2 * t) * GRID_W
                            segs = [(q_t, kT[hp:hp + HD, hc, 0:T], T, table[:, h - h0, a:a + T])] + segs
                            keys = list(range(TA))
                        units.append(Unit(segs=segs, pv=[v[:, s, h * HD:(h + 1) * HD] for s in keys],
                                                     out=o[:, t, h * HD:(h + 1) * HD]))
                attention(M, sa, units, 2, T + CTX, True)
        products(M, f"na_oT{l}", transposes(M, lambda t, j: o[:, t, j * P:(j + 1) * P],
                                            lambda j, a, n: yT[:, j, a * P:(a + n) * P], tq, 4))


def residual(x, gt):
    def ev(eng, bank, link, t, half):
        cols = slice(half * BANK, (half + 1) * BANK)
        link(eng.tensor_tensor(bank, bank, gt[:, 0 if t < TT else 1, cols], ALU.mult))
        return eng.tensor_tensor(x[:, t, cols], x[:, t, cols], bank, ALU.add)
    return ev


def stream_rows(M, l, after, t):
    if t < TT:
        return M.x_lat[t * P:(t + 1) * P, :]
    src = M.A["ctx_2"][0] if l == 0 and not after else M.x_ctx
    return src[(t - TT) * P:(t - TT + 1) * P, :]


def mlp(M, L, l, last):
    nc, tq = M.nc, L.tq
    streams = 1 if tq == TT else 2
    with Stage(nc, f"mlp{l}") as st:
        hidden = st.sb("hidden", [P, DFF // P, tq * P])
        hT = st.sb("hT", [P, DK, tq * P])
        gt = st.sb("gt", [P, streams, D])
        x = hidden[:, 0:DK, :].rearrange("p k n -> p (k n)").rearrange("p (t d) -> p t d", d=D)
        rms_rows(M, f"rms2_{l}", x, tq, 1, D,
                 load=lambda sp, t: sp.dma_start(x[:, t, :], stream_rows(M, l, True, t)), sq=gt[:, 0:1, :])
        modulated(M, L, f"h2_{l}", tq, x, L.gain2, 3 * DK, hT)
        gate_rows(M, f"gt2_{l}", L.mod, 5 * DK, streams, gt)
        t0 = M.weights.taken
        gs = []
        for c in range(DFF // P):
            def ev(eng, bank, link, r0, n, c=c):
                dst = hidden[:, c, r0:r0 + n]
                if on_scalar(eng):
                    link(eng.activation(dst, bank, ACT.Relu))
                    return eng.activation(dst, dst, ACT.Square)
                link(eng.tensor_scalar(dst, bank, 0.0, None, ALU.max))
                return eng.tensor_tensor(dst, dst, dst, ALU.mult)
            gs += column_groups(M, t0 + c // 4, (c % 4) * P, P, hT, None, "vs"[c % 2], rows=tq * P, evac=ev)
        products(M, f"ff1_p{l}", gs, tiles=8)
        x = hT[:, :, :].rearrange("p k n -> p (k n)").rearrange("p (t d) -> p t d", d=D)
        sig, W = st.sig, M.weights
        t0, base = W.taken, M.groups
        W.taken += 8
        ev = residual(x, gt)
        for half in range(2):
            for k in range(4):
                W.last_group[t0 + 4 * half + k] = base + 4 * half + k + 1
        M.groups += 8

        def bank_of(half, t):
            return (half * tq + t) % BANKS
        with nc.Block() as block:
            @block.sync
            def _(sp):
                for t in range(tq):
                    sp.dma_start(x[:, t, :], stream_rows(M, l, True, t)).then_inc(sig["x"], 16)
                W.load(sp, W.taken + RING)
                sp.wait_ge(sig["moved"], 2 * tq)
                for t in range(tq):
                    dst = M.out[0, t * P:(t + 1) * P, :] if last else stream_rows(M, l, True, t)
                    sp.dma_start(dst, x[:, t, :]).then_inc(sig["saved"], 16)
                sp.wait_ge(sig["saved"], 16 * tq)

            @block.tensor
            def _(pe):
                for half in range(2):
                    for k in range(4):
                        i = 4 * half + k
                        w = W.view(t0 + i)
                        W.arrived(pe, t0 + i)
                        for t in range(tq):
                            n = half * tq + t
                            if k == 0 and n >= BANKS:
                                pe.wait_ge(sig["moved"], n - BANKS + 1)
                            for j in range(DK):
                                last_ = pe.matmul(M.ps[:, bank_of(half, t), :],
                                                  hidden[:, k * DK + j, t * P:(t + 1) * P], w[:, j, :],
                                                  start=(k == 0 and j == 0), stop=(k == 3 and j == DK - 1))
                            if k == 3 and t < tq - 1:
                                last_.then_inc(sig["summed"], 1)
                        last_.then_inc(W.groups_done, 1)

            @block.vector
            def _(dve):
                link = Chain(dve, sig["chain"])
                dve.wait_ge(sig["x"], 16 * tq)
                for half in range(2):
                    for t in range(tq):
                        if t < tq - 1:
                            dve.wait_ge(sig["summed"], half * (tq - 1) + t + 1)
                        else:
                            dve.wait_ge(W.groups_done, base + 4 * half + 4)
                        ev(dve, M.ps[:, bank_of(half, t), :], link, t, half).then_inc(sig["moved"], 1)


def second_block(M):
    nc, A = M.nc, M.A
    for l in range(LAYERS):
        last = l == LAYERS - 1
        with Stage(nc, f"layer{l}") as st:
            L = Layer(TT if last else TA)
            L.mod = st.sb("mod", [P, 6 * DK, 2])
            L.gain1 = st.sb("gain1", [P, DK, 2])
            L.gain2 = st.sb("gain2", [P, DK, 2])
            streams = 1 if last else 2
            ada(M, L, l)
            with Stage(nc, f"mix{l}") as sm:
                hT = sm.sb("hT", [P, DK, TA * P])
                with Stage(nc, f"norm1_{l}") as sn:
                    x = sn.sb("x", [P, TA, D])
                    rms_rows(M, f"rms1_{l}", x, TA, 1, D,
                             load=lambda sp, t: sp.dma_start(x[:, t, :], stream_rows(M, l, False, t)))
                    modulated(M, L, f"h1_{l}", TA, x, L.gain1, 0, hT)
                yT = [sm.sb("y0T", [P, 4, L.tq * P])]
                latent_attention(M, L, l, hT, yT[0])
                yT.append(sm.sb("y1T", [P, 4, L.tq * P]))
                neighbourhood_attention(M, L, l, hT, yT[1])
                with Stage(nc, f"merge{l}") as sg:
                    merged = sg.sb("merged", [P, L.tq, D])
                    merge(M, f"merge2_{l}", hT, yT, merged, L.tq)
                    products(M, f"mergedT{l}", transposes(
                        M, lambda t, j: merged[:, t, j * P:(j + 1) * P],
                        lambda j, a, n: hT[:, j, a * P:(a + n) * P], L.tq, DK))
                with Stage(nc, f"wout{l}") as so:
                    x = so.sb("x", [P, L.tq, D])
                    gt = so.sb("gt", [P, streams, D])
                    gate_rows(M, f"gt1_{l}", L.mod, 2 * DK, streams, gt)
                    ev = residual(x, gt)
                    t0 = M.weights.taken

                    def load(sp):
                        for t in range(L.tq):
                            sp.dma_start(x[:, t, :], stream_rows(M, l, False, t)).then_inc(so.sig["x"], 16)
                    gs = []
                    for half in range(2):
                        def evac(eng, bank, link, t, half=half):
                            if half == 0 and t == 0:
                                eng.wait_ge(so.sig["x"], 16 * L.tq)
                            return ev(eng, bank, link, t, half)
                        gs += row_groups(M, t0 + half, 0, BANK, hT, None, on="v", rows=L.tq * P, evac=evac)
                    products(M, f"wout_p{l}", gs, tiles=2, extra={"sync": load})
                    with nc.Block() as block:
                        @block.sync
                        def _(sp):
                            for t in range(L.tq):
                                sp.dma_start(stream_rows(M, l, True, t), x[:, t, :]
                                             ).then_inc(so.sig["saved"], 16)
                            sp.wait_ge(so.sig["saved"], 16 * L.tq)
            mlp(M, L, l, last)


def program(nc, A, out):
    M = Machine(nc, A, out)
    with ExitStack() as ctx:
        def sb(name, shape, dt=F32):
            return ctx.enter_context(nc.sbuf_tensor(name, shape, dt))
        M.ps = ctx.enter_context(nc.psum_tensor("ps", [P, BANKS, BANK], F32))
        ring = sb("ring", [P, RING, TILE])
        w_in = A["w_in"][0]
        tiles = weight_tiles(w_in, 0, OFF_B)
        tiles += weight_tiles(w_in, OFF_B, OFF_C)
        tiles += weight_tiles(w_in, OFF_C, OFF_DZ)
        tiles += weight_tiles(w_in, OFF_DZ, OFF_GATES)
        for n in range(4):
            g = weight_tiles(w_in, OFF_GATES + n * D, OFF_GATES + (n + 1) * D)
            tiles += [g[0]] + weight_tiles(A["w_branch"][0, n], 0, D, D) + [g[1]]
        tiles += weight_tiles(A["w_out"][0], 0, D)
        tiles += second_tiles(A)
        M.x_ctx = nc.dram_tensor("x_ctx", [CTX, D], F32).ap()
        M.rpb_pad = nc.dram_tensor("rpb_pad", [MH * RPB_H * RPB_W + 3 * GRID_W], F32).ap()
        M.weights = Weights(nc, ring, tiles, nc.alloc_semaphore(name="groups_done"))
        M.scratch_L = nc.dram_tensor("scratch_L", [4, T], F32).ap()
        M.x1 = nc.dram_tensor("x1_rows", [T, D], F32).ap()
        M.x_lat = nc.dram_tensor("x_lat", [T, D], F32).ap()
        M.slot_token = nc.dram_tensor("slot_token", [NBLK * EB, 1], I32).ap()
        M.y_slot = nc.dram_tensor("y_slot", [NBLK * EB, D], F32).ap()
        route = Route(sb("dest", [P, 2, TT], I32), sb("gate", [P, 2, TT]), sb("expert", [1, NBLK + 2], I32))
        M.ident = sb("ident", [P, P])
        M.ones = sb("ones", [P, P])
        M.causal = sb("causal", [P, P])
        with Stage(nc, "const") as st:
            layer_constants(M, st)
        with Stage(nc, "mixers") as st:
            M.xT = st.sb("xT", [P, DK, T])
            oT = M.oT = [st.sb(f"o{n}T", [P, 2, T]) for n in range(4)]
            with Stage(nc, "x") as sx:
                load_x(M, sx)
            branch_a(M, oT[0])
            branch_b(M, oT[1])
            branch_c(M, oT[2])
            branch_d(M, oT[3])
            merged = st.sb("merged", [P, TT, D])
            merge(M, "merge", M.xT, oT, merged)
            mixer_out(M, merged)
            router(M, route)
        experts(M, route)
        combine(M, route)
        second_block(M)



_COLUMNS = ["c_w0", "c_a0", "c_kk", "c_ka", "c_rk", "c_mu", "d_conv_b", "c_2", "c_ctx_2"]
_LAYER_COLUMNS = ["b_ada_2", "g_attn_2", "g_mlp_2", "g_qa_2", "g_kva_2"]


def rope_tables():
    import numpy as np

    t = np.arange(T)
    freq = np.float32(10000.0) ** (-np.arange(8, dtype=np.float32) / 8)
    angles = np.stack([(t // GRID_W).astype(np.float32)[:, None] * freq,
                       (t % GRID_W).astype(np.float32)[:, None] * freq], axis=1)
    angles = angles.reshape(TT, P, 2, 8).transpose(1, 0, 2, 3)
    return np.cos(angles), np.sin(angles)


def arrays(inputs):
    import numpy as np

    out = {}
    for name, a in inputs.items():
        a = np.asarray(a)
        if a.size == 0:
            continue
        if name in _COLUMNS:
            a = a.reshape(-1, P).T
        if name in _LAYER_COLUMNS:
            a = a.reshape(LAYERS, -1, P).transpose(0, 2, 1)
        if name == "d_conv_w":
            a = a[0].reshape(4, 4, P).transpose(2, 1, 0)
        out[name] = np.ascontiguousarray(a)
    out["rope_cos"], out["rope_sin"] = (np.ascontiguousarray(a) for a in rope_tables())
    return out


def kernel(**inputs):
    import concourse.bacc as bacc
    from concourse.bass_utils import run_bass_kernel_spmd

    nc = bacc.Bacc("TRN2", target_bir_lowering=False, num_devices=1)
    ins = {"in_" + name: a for name, a in arrays(inputs).items()}
    aps = {name[3:]: nc.dram_tensor(name, a.shape, mybir.dt.from_np(a.dtype), kind="ExternalInput").ap()
           for name, a in ins.items()}
    out = nc.dram_tensor("out_0", (1, T, D), F32, kind="ExternalOutput").ap()
    program(nc, aps, out)
    return run_bass_kernel_spmd(nc, [ins], core_ids=[0]).results[0]["out_0"]
```
